# Optimizing a Trainium2 kernel written in Bass

```python
import jax, jax.numpy as jnp
from jax import lax
import numpy as np

D_MODEL = 1024
BATCH = 1
SEQ = 1024
DEPTH = 2

GRID_W = 64
CTX_LEN = 256
N_MIXERS = 2
D_RNN = 1024
RG_HEADS = 8
RG_BLOCK = D_RNN // RG_HEADS
RG_CONV = 4
RG_C = 8.0
POOL_WINDOWS = (2, 4, 8, 16)
N_POOL_GROUPS = len(POOL_WINDOWS)
POOL_GROUP = D_MODEL // N_POOL_GROUPS
D_FF = 3 * D_MODEL
FFN_CONV = 3
N_MOD = 6
N_RG_LAYERS = (DEPTH + 1) // 2
N_POOL_LAYERS = DEPTH // 2
EPS = 1e-6

kernel_name = "hybrid_rglru_pool_dit_trunk"

def _rms_norm(x, g):
    xf = x.astype(jnp.float32)
    y = xf * lax.rsqrt(jnp.mean(xf * xf, axis=-1, keepdims=True) + EPS)
    return (y * g.astype(jnp.float32)).astype(x.dtype)

def _modulate(h, shift, scale):
    return h * (1.0 + scale) + shift

def _dwconv(x, w, b, pad):
    c = x.shape[-1]
    y = lax.conv_general_dilated(x, w.astype(x.dtype)[:, None, :], window_strides=(1,), padding=(pad,),
                                 dimension_numbers=("NWC", "WIO", "NWC"), feature_group_count=c)
    return y + b.astype(x.dtype)

def _linear_scan(a, b, h0, reverse):
    if reverse:
        b = b.at[:, -1].add(a[:, -1] * h0)
    else:
        b = b.at[:, 0].add(a[:, 0] * h0)

    def comb(l, r):
        return l[0] * r[0], r[0] * l[1] + r[1]

    _, h = lax.associative_scan(comb, (a, b), reverse=reverse, axis=1)
    return h

def _rg_lru_terms(u, wa, ba, wx, bx, lam):
    bsz, n, _ = u.shape
    uh = u.reshape(bsz, n, RG_HEADS, RG_BLOCK)
    r = jax.nn.sigmoid((jnp.einsum("bthi,hij->bthj", uh, wa.astype(u.dtype)).reshape(bsz, n, D_RNN)
                        + ba.astype(u.dtype)).astype(jnp.float32))
    i = jax.nn.sigmoid((jnp.einsum("bthi,hij->bthj", uh, wx.astype(u.dtype)).reshape(bsz, n, D_RNN)
                        + bx.astype(u.dtype)).astype(jnp.float32))
    log_a = -RG_C * r * jax.nn.softplus(-lam.astype(jnp.float32))
    mult = jnp.sqrt(-jnp.expm1(2.0 * log_a))
    return jnp.exp(log_a), mult * (i * u.astype(jnp.float32))

def _rglru_mixer(h_ctx, h_lat, w_in, conv_w, conv_b, wa, ba, wx, bx, lam, w_out, need_ctx_out):
    def branches(h):
        z = h @ w_in.astype(h.dtype)
        g, rec = z[..., :D_RNN], z[..., D_RNN:]
        u = _dwconv(rec, conv_w, conv_b, (RG_CONV // 2, RG_CONV - 1 - RG_CONV // 2))
        return jax.nn.gelu(g), u

    g_ctx, u_ctx = branches(h_ctx)
    g_lat, u_lat = branches(h_lat)
    bsz = h_lat.shape[0]
    y_ctx = jnp.zeros(u_ctx.shape, jnp.float32)
    y_lat = jnp.zeros(u_lat.shape, jnp.float32)
    for d, rev in enumerate((False, True)):
        a_c, b_c = _rg_lru_terms(u_ctx, wa[d], ba[d], wx[d], bx[d], lam[d])
        hc = _linear_scan(a_c, b_c, jnp.zeros((bsz, D_RNN), jnp.float32), rev)
        h_final = hc[:, 0] if rev else hc[:, -1]
        a_l, b_l = _rg_lru_terms(u_lat, wa[d], ba[d], wx[d], bx[d], lam[d])
        y_lat = y_lat + _linear_scan(a_l, b_l, h_final, rev)
        if need_ctx_out:
            y_ctx = y_ctx + hc
    out_lat = (g_lat * y_lat.astype(h_lat.dtype)) @ w_out.astype(h_lat.dtype)
    out_ctx = (g_ctx * y_ctx.astype(h_ctx.dtype)) @ w_out.astype(h_ctx.dtype) if need_ctx_out else None
    return out_ctx, out_lat

def _window_sum(x, w, axis):
    n = x.shape[axis]
    cs = jnp.cumsum(x, axis=axis)
    s = jnp.concatenate([jnp.zeros_like(lax.slice_in_dim(cs, 0, 1, axis=axis)), cs], axis=axis)
    t = jnp.arange(n)
    lo = jnp.clip(t - w // 2, 0, n)
    hi = jnp.clip(t + w // 2, 0, n)
    win = jnp.take(s, hi, axis=axis) - jnp.take(s, lo, axis=axis)
    cnt = (hi - lo).astype(jnp.float32).reshape((n,) + (1,) * (x.ndim - axis - 1))
    return win, cnt

def _pool_mixer(h, w_grp, b, scale, rows):
    hf = h.astype(jnp.float32)
    bsz, n, _ = h.shape
    outs = []
    for g, w in enumerate(POOL_WINDOWS):
        hg = hf[..., g * POOL_GROUP:(g + 1) * POOL_GROUP]
        if rows is None:
            s, cnt = _window_sum(hg, w, 1)
            pooled = s / cnt
        else:
            hg2 = hg.reshape(bsz, rows, GRID_W, POOL_GROUP)
            s, cr = _window_sum(hg2, w, 1)
            s, cc = _window_sum(s, w, 2)
            pooled = (s / (cr * cc)).reshape(bsz, n, POOL_GROUP)
        outs.append(jnp.einsum("btc,cd->btd", (pooled - hg).astype(h.dtype), w_grp[g].astype(h.dtype)))
    y = jnp.concatenate(outs, axis=-1) + b.astype(h.dtype)
    return y * scale.astype(h.dtype)

def _conv_ffn(h, w_up, conv_w, conv_b, w_down):
    z = h @ w_up.astype(h.dtype)
    u, v = z[..., :D_FF], z[..., D_FF:]
    u = _dwconv(u, conv_w, conv_b, (FFN_CONV // 2, FFN_CONV // 2))
    return (jax.nn.gelu(u) * v) @ w_down.astype(h.dtype)

def setup_inputs(seed: int = 0) -> dict:
    key = jax.random.key(seed)
    ks = iter(jax.random.split(key, 32))
    f32 = jnp.float32

    def nrm(shape, scale):
        return jax.random.normal(next(ks), shape, f32) * scale

    a0 = jax.random.uniform(next(ks), (N_RG_LAYERS, 2, D_RNN), f32, 0.9, 0.999)
    return {
        "x": nrm((BATCH, SEQ, D_MODEL), 1.0),
        "c": nrm((BATCH, D_MODEL), 1.0),
        "ctx": nrm((BATCH, CTX_LEN, D_MODEL), 1.0),
        "c_ctx": nrm((D_MODEL,), 1.0),
        "ada_w": nrm((DEPTH, D_MODEL, N_MOD * D_MODEL), 0.5 * D_MODEL ** -0.5),
        "ada_b": nrm((DEPTH, N_MOD * D_MODEL), 0.01),
        "norm_pre_mix": 1.0 + nrm((DEPTH, D_MODEL), 0.05),
        "norm_post_mix": 1.0 + nrm((DEPTH, D_MODEL), 0.05),
        "norm_pre_ffn": 1.0 + nrm((DEPTH, D_MODEL), 0.05),
        "norm_post_ffn": 1.0 + nrm((DEPTH, D_MODEL), 0.05),
        "rg_w_in": nrm((N_RG_LAYERS, D_MODEL, 2 * D_RNN), D_MODEL ** -0.5),
        "rg_conv_w": nrm((N_RG_LAYERS, RG_CONV, D_RNN), RG_CONV ** -0.5),
        "rg_conv_b": nrm((N_RG_LAYERS, D_RNN), 0.01),
        "rg_gate_a_w": nrm((N_RG_LAYERS, 2, RG_HEADS, RG_BLOCK, RG_BLOCK), RG_BLOCK ** -0.5),
        "rg_gate_a_b": nrm((N_RG_LAYERS, 2, D_RNN), 0.01),
        "rg_gate_x_w": nrm((N_RG_LAYERS, 2, RG_HEADS, RG_BLOCK, RG_BLOCK), RG_BLOCK ** -0.5),
        "rg_gate_x_b": nrm((N_RG_LAYERS, 2, D_RNN), 0.01),
        "rg_lambda": jnp.log(a0) - jnp.log1p(-a0),
        "rg_w_out": nrm((N_RG_LAYERS, D_RNN, D_MODEL), D_RNN ** -0.5),
        "pool_w": nrm((N_POOL_LAYERS, N_POOL_GROUPS, POOL_GROUP, POOL_GROUP), POOL_GROUP ** -0.5),
        "pool_b": nrm((N_POOL_LAYERS, D_MODEL), 0.01),
        "pool_scale": 1.0 + nrm((N_POOL_LAYERS, D_MODEL), 0.1),
        "ffn_w_up": nrm((DEPTH, D_MODEL, 2 * D_FF), D_MODEL ** -0.5),
        "ffn_conv_w": nrm((DEPTH, FFN_CONV, D_FF), FFN_CONV ** -0.5),
        "ffn_conv_b": nrm((DEPTH, D_FF), 0.01),
        "ffn_w_down": nrm((DEPTH, D_FF, D_MODEL), D_FF ** -0.5),
    }

def reference(x, c, ctx, c_ctx, ada_w, ada_b, norm_pre_mix, norm_post_mix, norm_pre_ffn, norm_post_ffn,
              rg_w_in, rg_conv_w, rg_conv_b, rg_gate_a_w, rg_gate_a_b, rg_gate_x_w, rg_gate_x_b,
              rg_lambda, rg_w_out, pool_w, pool_b, pool_scale, ffn_w_up, ffn_conv_w, ffn_conv_b,
              ffn_w_down):
    rows = x.shape[1] // GRID_W
    sc = jax.nn.silu(c)
    sc_ctx = jax.nn.silu(c_ctx)
    for i in range(DEPTH):
        last = i == DEPTH - 1
        mod_l = jnp.split((sc @ ada_w[i] + ada_b[i])[:, None, :], N_MOD, axis=-1)
        mod_c = jnp.split(sc_ctx @ ada_w[i] + ada_b[i], N_MOD, axis=-1)
        sh_m, sc_m, g_m, sh_f, sc_f, g_f = mod_l
        csh_m, csc_m, cg_m, csh_f, csc_f, cg_f = mod_c

        h_lat = _modulate(_rms_norm(x, norm_pre_mix[i]), sh_m, sc_m)
        h_ctx = _modulate(_rms_norm(ctx, norm_pre_mix[i]), csh_m, csc_m)
        j = i // N_MIXERS
        if i % N_MIXERS == 0:
            y_ctx, y_lat = _rglru_mixer(h_ctx, h_lat, rg_w_in[j], rg_conv_w[j], rg_conv_b[j],
                                        rg_gate_a_w[j], rg_gate_a_b[j], rg_gate_x_w[j], rg_gate_x_b[j],
                                        rg_lambda[j], rg_w_out[j], not last)
        else:
            y_lat = _pool_mixer(h_lat, pool_w[j], pool_b[j], pool_scale[j], rows)
            y_ctx = None if last else _pool_mixer(h_ctx, pool_w[j], pool_b[j], pool_scale[j], None)
        x = x + g_m * _rms_norm(y_lat, norm_post_mix[i])
        if not last:
            ctx = ctx + cg_m * _rms_norm(y_ctx, norm_post_mix[i])

        f_lat = _conv_ffn(_modulate(_rms_norm(x, norm_pre_ffn[i]), sh_f, sc_f),
                          ffn_w_up[i], ffn_conv_w[i], ffn_conv_b[i], ffn_w_down[i])
        x = x + g_f * _rms_norm(f_lat, norm_post_ffn[i])
        if not last:
            f_ctx = _conv_ffn(_modulate(_rms_norm(ctx, norm_pre_ffn[i]), csh_f, csc_f),
                              ffn_w_up[i], ffn_conv_w[i], ffn_conv_b[i], ffn_w_down[i])
            ctx = ctx + cg_f * _rms_norm(f_ctx, norm_post_ffn[i])
    return x


_drawn_inputs = setup_inputs


def setup_inputs(seed=0):
    import zlib

    import numpy as np

    out = dict(_drawn_inputs(seed))
    spreads = {}
    factors = {'ctx': 4.244,
     'norm_post_mix': 2.679,
     'norm_post_ffn': 2.917,
     'rg_conv_b': 6.093,
     'rg_gate_a_b': 39.289,
     'rg_gate_x_b': 23.543,
     'pool_b': 8.0,
     'ffn_conv_b': 8.0}
    for name, (base, spread) in spreads.items():
        noise = np.random.default_rng([zlib.crc32(name.encode()), seed]).standard_normal(out[name].shape)
        drawn = base * np.exp(spread * noise) if base else spread * noise
        out[name] = __import__('jax').numpy.asarray(drawn.astype(out[name].dtype))
    for name, factor in factors.items():
        out[name] = (out[name] * factor).astype(out[name].dtype)
    return out
```

```python
from contextlib import ExitStack

import concourse.bass as bass
from concourse import mybir

P = 128
D = 1024
T = 1024
NC_ = 256
KT = D // P
HF = 512
NH = 8
FJ = 3 * D // P
GW = 64
GR = T // GW
WINDOWS = (2, 4, 8, 16)
EPS = 1e-6
RG_C = 8.0

LAT = NC_ + 2
TA = LAT + T

_COLS = {}
_at = 0
for _name, _n in (("ada_b", 96), ("npre_mix", 16), ("npost_mix", 16), ("npre_ffn", 16), ("npost_ffn", 16),
                  ("rg_conv_w", 32), ("rg_conv_b", 8), ("gate_a_b", 16), ("gate_x_b", 16), ("lam", 16),
                  ("pool_b", 8), ("pool_scale", 8), ("ffn_conv_w", 144), ("ffn_conv_b", 48), ("cond", 16)):
    _COLS[_name] = _at
    _at += _n
NPAR = _at

ADA0 = 16
START_UNITS = 8
START_A = 5
N_WOUT = NH
N_FFN = (NH + 4, NH + 4 + FJ + 1)
N_POOL = NH + 4 + FJ
N_AB = N_FFN[1] + FJ

F32 = mybir.dt.float32
F32R = mybir.dt.float32r
ALU = mybir.AluOpType
ACT = mybir.ActivationFunctionType


def build_trunk(nc, xT, ctxT, params, ada, wA, wB, wC, gatew, poolcnt, ident_in, outT):
    with ExitStack() as top:
        def sb(name, shape, dt=F32, scope=top):
            return scope.enter_context(nc.sbuf_tensor(name, shape, dt))

        def sem(name):
            return top.enter_context(nc.semaphore(name))

        H_hi = sb("H_hi", [P, KT, T], F32R)
        H_lo = sb("H_lo", [P, KT, T], F32R)
        Y = sb("Y", [P, KT, T])
        slots = ("A", "B", "C")
        raw = {s: sb(f"raw{s}", [P, D]) for s in slots}
        W_hi = {s: sb(f"W{s}_hi", [P, D], F32R) for s in slots}
        W_lo = {s: sb(f"W{s}_lo", [P, D], F32R) for s in slots}
        E = [sb(f"ada_raw{i}", [P, KT, P]) for i in range(2)]
        S = [sb(f"S{i}", [P, T]) for i in range(2)]
        F_hi = sb("F_hi", [P, T], F32R)
        F_lo = sb("F_lo", [P, T], F32R)
        par = sb("par", [P, NPAR])
        M = sb("M", [P, 96])
        Mc = sb("Mc", [P, ADA0])
        silu_c = sb("silu_c", [P, KT, 2])
        cA = sb("cA", [P, 4, KT])
        cAc = sb("cAc", [P, KT])
        cG = sb("cG", [P, 4, KT])
        pbs = sb("pbs", [P, KT])
        ident = sb("ident", [P, P])
        ones = sb("ones", [P, P])
        eps = sb("eps", [P, 1])
        rms = sb("rms", [P, KT])
        rstd = sb("rstd", [P, KT])
        rms_c = sb("rms_c", [P, 2])
        rstd_c = sb("rstd_c", [P, 2])
        sp = sb("sp", [P, 8, 2 * NH])
        s_tanh = sb("s_tanh", [P, 2 * NH])
        s_exp = sb("s_exp", [P, 2 * NH])

        def overlay(*plan):
            with ExitStack() as scope:
                out = []
                for n, item in enumerate(plan):
                    if isinstance(item, tuple):
                        out.append(sb(*item, scope=scope))
                    else:
                        sb(f"gap_{plan[-1][0]}_{n}", [P, int(item * 256)], scope=scope)
            return out

        ctx_x, ctx_sq, ada_a, ada_b2, diag_c = overlay(
            ("ctx_x", [P, KT, NC_]), ("ctx_sq", [P, KT, NC_]), ("ada_a", [P, START_A, D]), 13,
            ("ada_b2", [P, START_UNITS - START_A, D]), ("diag_c", [P, 2, P]))
        rec, u, RA0, Hc_hi, Hc_lo, RA1, IB0, IB1, TH0, TH1, gw = overlay(
            ("rec", [P, TA + 3]), ("u", [P, TA]), ("RA0", [P, TA]), 1.25,
            ("Hc_hi", [P, KT, NC_], F32R), ("Hc_lo", [P, KT, NC_], F32R), ("RA1", [P, TA]),
            ("IB0", [P, TA]), ("IB1", [P, TA]), ("TH0", [P, TA]), ("TH1", [P, TA]), ("gw", [P, 4, P]))
        RA, IB, TH = (RA0, RA1), (IB0, IB1), (TH0, TH1)
        X, Ub, acc0, acc1, diag = overlay(
            ("X", [P, KT, T]), ("Ub", [P, T + 2]), ("acc0", [P, T]), ("acc1", [P, T]), ("diag", [P, KT, P]))
        acc = (acc0, acc1)
        col_x, row_x, pt0, pt1 = overlay(
            32, ("col_x", [P, GR, GW + 16]), ("row_x", [P, GR + 16, GW]),
            ("pt0", [P, (GR + 16) * GW]), ("pt1", [P, (GR + 16) * GW]))
        pt = (pt0, pt1)
        ps = top.enter_context(nc.psum_tensor("ps", [P, 8, 512], F32))
        AB01, AB23, AB45, AB67 = (ps[:, b:b + 2, :] for b in (0, 2, 4, 6))

        par_full, ctx_full, const_full = sem("par_full"), sem("ctx_full"), sem("const_full")
        x_full = [sem(f"x_full{q}") for q in range(4)]
        res_full = [sem(f"res_full{q}") for q in range(4)]
        ada_start_full = [sem(f"ada_start_full{q}") for q in range(2)]
        e_full = [sem(f"ada_full{i}") for i in range(2)]
        raw_full = {s: sem(f"raw_full_{s}") for s in slots}
        w_hi = {s: sem(f"w_hi_{s}") for s in slots}
        w_ready = {s: sem(f"w_ready_{s}") for s in slots}
        unit_done = {s: sem(f"unit_done_{s}") for s in "AB"}
        gw_full, gate_done, gate_evac = sem("gw_full"), sem("gate_done"), sem("gate_evac")
        memset_done, zeros_ready, y_zero = sem("memset_done"), sem("zeros_ready"), sem("y_zero")
        silu_done, softplus_step, lam_ready = sem("silu_done"), sem("softplus_step"), sem("lam_ready")
        ada_out, ada_added, coef_ready = sem("ada_out"), sem("ada_added"), sem("coef_ready")
        sq_made, sum_even, sum_odd = sem("sq_made"), sem("sum_even"), sem("sum_odd")
        ssq_done, rms_made, rstd_made = sem("ssq_done"), sem("rms_made"), sem("rstd_made")
        diag_made, rb_done = sem("diag_made"), sem("rb_done")
        csq_made, cssq_done, crms_made = sem("ctx_sq_made"), sem("ctx_ssq_done"), sem("ctx_rms_made")
        crstd_made, cdiag_made, crb_done = sem("ctx_rstd_made"), sem("ctx_diag_made"), sem("ctx_rb_done")
        cscaled, caffine, chi, hc_ready = sem("ctx_scaled"), sem("ctx_affine"), sem("ctx_hi"), sem("ctx_h_ready")
        x_scaled, affine_made, h_hi, h_ready = sem("x_scaled"), sem("affine_made"), sem("h_hi"), sem("h_ready")
        y_scaled, x_new, y_evac = sem("y_scaled"), sem("x_new"), sem("y_evac")
        rec_evac, conv_step, u_made = sem("rec_evac"), sem("conv_step"), sem("u_made")
        g_made, tanh_made, exp_made, sqrt_made = sem("g_made"), sem("tanh_made"), sem("exp_made"), sem("sqrt_made")
        mult_made, iu_made, b_made = sem("mult_made"), sem("iu_made"), sem("b_made")
        scan_ctx, scan_done, ysum_made, gy_made = sem("scan_ctx"), sem("scan_done"), sem("ysum_made"), sem("gy_made")
        u_evac, tap_done, conv_a, conv_done = sem("u_evac"), sem("tap_done"), sem("conv_a"), sem("conv_done")
        gelu_done, f_mul, f_hi, f_ready = sem("gelu_done"), sem("f_mul"), sem("f_hi"), sem("f_ready")
        d_done, d_added = sem("d_done"), sem("d_added")
        pads_ready, col_loaded, pool_step = sem("pads_ready"), sem("col_loaded"), sem("pool_step")
        cnt_full = [sem(f"cnt_full{i}") for i in range(2)]
        diff_made, pool_mm, out_done = sem("diff_made"), sem("pool_mm"), sem("out_done")

        block = top.enter_context(nc.Block())

        def col(name, n=0, w=1):
            c = _COLS[name] + n
            return par[:, bass.ds(c, w)]

        def flat(banks):
            return banks.rearrange("p a b -> p (a b)")

        @block.sync
        def _(sp_):
            def load_raw(s, n):
                if not (isinstance(n, int) and n == 0):
                    sp_.wait_ge(w_ready[s], n)
                sp_.dma_start(raw[s][:], {"A": wA, "B": wB, "C": wC}[s][n]).then_inc(raw_full[s], 16)

            def load_pair(p):
                if not (isinstance(p, int) and p == 0):
                    sp_.wait_ge(ada_out, p)
                for i in range(2):
                    sp_.dma_start(E[i][:], ada[START_UNITS + 2 * p + i].rearrange("p (k m) -> p k m", k=KT))\
                       .then_inc(e_full[i], 16)

            sp_.dma_start(par[:], params).then_inc(par_full, 16)
            sp_.dma_start(ident[:], ident_in).then_inc(const_full, 16)
            sp_.dma_start(ctx_x[:], ctxT).then_inc(ctx_full, 16)
            for q in range(4):
                sp_.dma_start(Y[:, 2 * q:2 * q + 2], xT[:, 2 * q:2 * q + 2]).then_inc(x_full[q], 16)
                if q == 0:
                    sp_.dma_start(ada_a[:], ada[0:START_A].rearrange("u p c -> p u c"))\
                       .then_inc(ada_start_full[0], 16)
                if q == 1:
                    sp_.dma_start(ada_b2[:], ada[START_A:START_UNITS].rearrange("u p c -> p u c"))\
                       .then_inc(ada_start_full[1], 16)
                load_pair(q)
            load_raw("A", 0)
            load_raw("B", 0)
            load_raw("A", 1)
            load_raw("B", 1)
            sp_.wait_ge(crb_done, 1)
            sp_.dma_start(gw[:], gatew[0]).then_inc(gw_full, 16)
            load_pair(4)

            def head_loads(hd, last=False):
                load_raw("A", hd + 2)
                load_raw("B", hd + 2)
                load_pair(2 * hd + 5)
                if not last:
                    sp_.wait_ge(gate_done, 4 * hd + 4)
                    sp_.dma_start(gw[:], gatew[hd + 1]).then_inc(gw_full, 16)
                load_pair(2 * hd + 6)

            head_loads(0)
            with sp_.Fori(1, NH - 1) as hd:
                head_loads(hd)
            head_loads(NH - 1, last=True)
            sp_.wait_ge(gy_made, NH)
            for q in range(4):
                sp_.dma_start(X[:, 2 * q:2 * q + 2], xT[:, 2 * q:2 * q + 2]).then_inc(res_full[q], 16)
            load_raw("C", 0)
            for i in range(4):
                load_raw("A", NH + 2 + i)
                load_raw("B", NH + 2 + i)

            def ffn_loads(L, j):
                n, c = N_FFN[L] + j, FJ * L + j
                static = isinstance(j, int)
                if not static or n + 2 < N_AB:
                    load_raw("A", n + 2)
                if L == 0 and not (static and j == FJ - 1):
                    load_pair(2 * NH + 4 + j + 1)
                if not static or c + 1 < 2 * FJ:
                    load_raw("C", c + 1)
                if not static or n + 2 < N_AB:
                    load_raw("B", n + 2)

            def ffn(L):
                ffn_loads(L, 0)
                with sp_.Fori(1, FJ - 2) as j:
                    ffn_loads(L, j)
                ffn_loads(L, FJ - 2)
                ffn_loads(L, FJ - 1)

            ffn(0)
            for g in range(4):
                if g < 2:
                    sp_.wait_ge(ssq_done, 5)
                else:
                    sp_.wait_ge(diff_made, 2 * (g - 1))
                sp_.dma_start(S[g % 2][:], poolcnt[g:g + 1, :].to_broadcast([P, T]))\
                   .then_inc(cnt_full[g % 2], 16)
            load_raw("A", N_POOL + 2)
            load_raw("B", N_POOL + 2)
            ffn(1)
            for m in range(KT):
                sp_.wait_ge(x_new, 8 * 3 + m + 1)
                sp_.dma_start(outT[:, m], X[:, m]).then_inc(out_done, 16)
            sp_.wait_ge(out_done, 16 * KT)

        @block.tensor
        def _(pe):
            def product(s, w_cols, pieces, h, first=True, last=True):
                for w, part in ((W_hi[s], 0), (W_hi[s], 1), (W_lo[s], 0)):
                    for out, hi, lo in pieces:
                        mm = pe.matmul(out, w[:, w_cols:w_cols + P], (hi, lo)[part],
                                       start=first and w is W_hi[s] and part == 0,
                                       stop=last and w is W_lo[s])
                return mm

            def halves(banks, hi, lo, k):
                return [(banks[:, h], hi[:, k, h * HF:(h + 1) * HF], lo[:, k, h * HF:(h + 1) * HF])
                        for h in range(2)]

            def unit(s, n, banks, fill=None, context=None):
                pe.wait_ge(w_ready[s], n + 1)
                for k in range(KT):
                    if fill is not None:
                        pe.wait_ge(h_ready, 8 * fill + k + 1)
                    pieces = halves(banks, H_hi, H_lo, k)
                    if context is not None:
                        pieces.append((context, Hc_hi[:, k], Hc_lo[:, k]))
                    mm = product(s, k * P, pieces, k, k == 0, k == KT - 1)
                mm.then_inc(unit_done[s], 1)

            def ada_pair(p, out):
                for i in range(2):
                    pe.wait_ge(e_full[i], 16 * p + 16)
                    for k in range(KT):
                        mm = pe.matmul(out[:, i:i + 1], E[i][:, k], silu_c[:, k, 0:1],
                                       start=k == 0, stop=k == KT - 1)
                mm.then_inc(ada_out, 1)

            def square_sums(q):
                pe.wait_ge(sum_even, 3 * (q + 1))
                pe.wait_ge(sum_odd, 3 * (q + 1))
                for t in range(KT):
                    for a in range(2):
                        mm = pe.matmul(ps[:, 4, t:t + 1], acc[a][:, t * P:(t + 1) * P], ones[:, 0:1],
                                       start=a == 0, stop=a == 1)
                mm.then_inc(ssq_done, 1)

            def spread(q):
                pe.wait_ge(diag_made, q + 1)
                for h in range(2):
                    mm = pe.matmul(AB67[:, h], ones[:], diag[:, 4 * h:4 * h + 4], start=True, stop=True)
                mm.then_inc(rb_done, 1)

            pe.wait_ge(silu_done, 1)
            for n in range(START_UNITS + 8):
                if n < START_UNITS:
                    pe.wait_ge(ada_start_full[n >= START_A], 16)
                    w = (ada_a[:, n] if n < START_A else ada_b2[:, n - START_A]).rearrange(
                        "p (k m) -> p k m", k=KT)
                else:
                    p, i = divmod(n - START_UNITS, 2)
                    pe.wait_ge(e_full[i], 16 * p + 16)
                    w = E[i]
                for k in range(KT):
                    mm = pe.matmul(ps[:, 2, 2 * n:2 * n + 2], w[:, k], silu_c[:, k],
                                   start=k == 0, stop=k == KT - 1)
                if n >= START_UNITS and n % 2:
                    mm.then_inc(ada_out, 1)
            pe.wait_ge(const_full, 16)
            pe.wait_ge(memset_done, 3)
            square_sums(0)
            pe.wait_ge(csq_made, 1)
            for t in range(2):
                for k in range(KT):
                    mm = pe.matmul(ps[:, 5, t:t + 1], ctx_sq[:, k, t * P:(t + 1) * P], ones[:, 0:1],
                                   start=k == 0, stop=k == KT - 1)
            mm.then_inc(cssq_done, 1)
            spread(0)
            pe.wait_ge(cdiag_made, 1)
            pe.matmul(ps[:, 3, 0:NC_], ones[:], diag_c[:], start=True, stop=True).then_inc(crb_done, 1)

            def rec_product(n, fill=None):
                unit("A", n, ps[:, 1:3, :], fill=fill, context=ps[:, 0, 0:NC_])

            def head(hd, last=False):
                first = isinstance(hd, int) and hd == 0
                if not first:
                    pe.wait_ge(gate_evac, 4 * hd - 1)
                ada_pair(2 * hd + 4, ps[:, 3, 0:2])
                if not first:
                    pe.wait_ge(ada_added, 2 * hd + 1)
                unit("B", hd, AB67)
                pe.wait_ge(gw_full, 16 * hd + 16)
                pe.wait_ge(u_made, hd + 1)
                for gi in range(4):
                    if gi == 0:
                        pe.wait_ge(ada_added, 2 * hd + 2)
                    elif gi == 1:
                        pe.wait_ge(rec_evac, hd + 1)
                    else:
                        pe.wait_ge(gate_evac, 4 * hd + gi - 1)
                    b = 3 if gi % 2 == 0 else 0
                    for out, src in ((ps[:, b, 0:NC_], u[:, 0:NC_]), (ps[:, b + 1], u[:, LAT:LAT + HF]),
                                     (ps[:, b + 2], u[:, LAT + HF:TA])):
                        mm = pe.matmul(out, gw[:, gi], src, start=True, stop=True)
                    mm.then_inc(gate_done, 1)
                pe.wait_ge(g_made, hd + 1)
                ada_pair(2 * hd + 5, ps[:, 6, 0:2])
                if not last:
                    pe.wait_ge(gate_evac, 4 * hd + 4)
                    rec_product(hd + 1)

            pe.wait_ge(hc_ready, 1)
            pe.wait_ge(ada_added, 1)
            rec_product(0, fill=0)
            head(0)
            with pe.Fori(1, NH - 1) as hd:
                head(hd)
            head(NH - 1, last=True)

            pe.wait_ge(gate_evac, 4 * NH)
            unit("A", NH, AB01, fill=1)
            unit("B", NH, AB23)
            with pe.Fori(1, 4) as i:
                pe.wait_ge(y_evac, 2 * i - 1)
                unit("A", NH + i, AB01)
                pe.wait_ge(y_evac, 2 * i)
                unit("B", NH + i, AB23)
            pe.wait_ge(ada_added, 2 * NH + 1)
            square_sums(1)
            spread(1)
            square_sums(2)
            spread(2)

            def down(L, j):
                c = FJ * L + j
                pe.wait_ge(w_ready["C"], c + 1)
                pe.wait_ge(f_ready, c + 1)
                for m in range(KT):
                    if m >= 2 or not (isinstance(c, int) and c == 0):
                        pe.wait_ge(d_added, 8 * c + m - 1)
                    b = 4 + 2 * (m % 2)
                    pieces = [(ps[:, b + h], F_hi[:, h * HF:(h + 1) * HF], F_lo[:, h * HF:(h + 1) * HF])
                              for h in range(2)]
                    product("C", m * P, pieces, 0).then_inc(d_done, 1)

            def ffn_step(L, j):
                n, c = N_FFN[L] + j, FJ * L + j
                at0 = isinstance(j, int) and j == 0
                if not at0:
                    pe.wait_ge(u_evac, c)
                    if L == 0:
                        pe.wait_ge(ada_added, 2 * NH + 1 + j)
                unit("A", n, AB01, fill=2 + 2 * L if at0 else None)
                if not at0:
                    down(L, j - 1)
                    pe.wait_ge(f_mul, c)
                    if L == 0:
                        pe.wait_ge(u_evac, c + 1)
                        ada_pair(2 * NH + 4 + j, ps[:, 0, 0:2])
                unit("B", n, AB23)
                if at0 and L == 0:
                    pe.wait_ge(u_evac, 1)
                    ada_pair(2 * NH + 4, ps[:, 0, 0:2])

            def ffn(L):
                ffn_step(L, 0)
                ffn_step(L, 1)
                with pe.Fori(2, FJ - 1) as j:
                    ffn_step(L, j)
                ffn_step(L, FJ - 1)
                down(L, FJ - 1)
                square_sums(3 + 4 * L)
                spread(3 + 4 * L)

            ffn(0)
            square_sums(4)
            spread(4)

            pe.wait_ge(ada_added, 2 * NH + 1 + FJ)
            for g in range(4):
                s = "A" if g < 2 else "B"
                pe.wait_ge(w_ready[s], N_POOL + 1)
                for m in range(2):
                    mt = 2 * g + m
                    if mt >= 2:
                        pe.wait_ge(y_evac, 8 + mt - 1)
                    banks = (AB01, AB23)[m]
                    for k in range(2):
                        pe.wait_ge(h_ready, 8 * 3 + 2 * g + k + 1)
                        mm = product(s, (g % 2) * 512 + k * 256 + m * P,
                                     halves(banks, H_hi, H_lo, 2 * g + k), k, k == 0, k == 1)
                    mm.then_inc(unit_done[s] if mt % 4 == 3 else pool_mm, 1)
            square_sums(5)
            spread(5)
            square_sums(6)
            spread(6)
            pe.wait_ge(y_evac, 16)
            ffn(1)

        @block.scalar
        def _(act):
            A = act.activation

            def round_hi(s, n):
                act.wait_ge(raw_full[s], 16 * n + 16)
                if not (isinstance(n, int) and n == 0):
                    if s == "C":
                        act.wait_ge(d_done, 8 * n)
                    else:
                        act.wait_ge(unit_done[s], n)
                A(W_hi[s][:], raw[s][:], ACT.Copy).then_inc(w_hi[s], 1)

            def square(q, m, src):
                if m < 2:
                    dst = acc[m]
                    if q:
                        act.wait_ge(ssq_done, q)
                else:
                    dst = S[m % 2]
                    if m >= 4:
                        act.wait_ge((sum_even, sum_odd)[m % 2], 3 * q + m // 2 - 1)
                A(dst[:], src, ACT.Square).then_inc(sq_made, 1)

            def norm_root(q):
                act.wait_ge(ssq_done, q + 1)
                A(rms[:], ps[:, 4, 0:KT], ACT.Sqrt, scale=1.0 / D, bias=eps[:, 0:1]).then_inc(rms_made, 1)

            def affine(i, k, src, L, ffn_part):
                act.wait_ge(x_scaled, 8 * i + k + 1)
                A(Y[:, k], src, ACT.Identity, scale=cA[:, i, k:k + 1],
                  bias=M[:, 48 * L + 24 * ffn_part + k:48 * L + 24 * ffn_part + k + 1]).then_inc(affine_made, 1)

            def hi_of(fill, k):
                A(H_hi[:, k], Y[:, k], ACT.Copy).then_inc(h_hi, 1)

            act.wait_ge(par_full, 16)
            A(silu_c[:], col("cond", 0, 16).rearrange("p (k v) -> p k v", v=2), ACT.Silu).then_inc(silu_done, 1)
            A(sp[:, 0], col("lam", 0, 16), ACT.Abs).then_inc(softplus_step, 1)
            act.wait_ge(softplus_step, 1)
            A(sp[:, 1], sp[:, 0], ACT.Exp, scale=-1.0).then_inc(softplus_step, 1)
            act.wait_ge(softplus_step, 3)
            A(sp[:, 3], sp[:, 2], ACT.Ln).then_inc(softplus_step, 1)
            for m in range(KT):
                act.wait_ge(x_full[m // 2], 16)
                square(0, m, Y[:, m])
            act.wait_ge(ctx_full, 16)
            A(ctx_sq[:], ctx_x[:], ACT.Square).then_inc(csq_made, 1)
            round_hi("A", 0)
            round_hi("B", 0)
            act.wait_ge(memset_done, 3)
            norm_root(0)
            act.wait_ge(cssq_done, 1)
            A(rms_c[:], ps[:, 5, 0:2], ACT.Sqrt, scale=1.0 / D, bias=eps[:, 0:1]).then_inc(crms_made, 1)
            act.wait_ge(coef_ready, 1)
            act.wait_ge(cscaled, 1)
            for k in range(KT):
                A(ctx_x[:, k], ctx_x[:, k], ACT.Identity, scale=cAc[:, k:k + 1], bias=Mc[:, k:k + 1])\
                    .then_inc(caffine, 1)
            act.wait_ge(caffine, KT)
            A(Hc_hi[:], ctx_x[:], ACT.Copy).then_inc(chi, 1)
            for k in range(KT):
                affine(0, k, Y[:, k], 0, 0)
                act.wait_ge(affine_made, k + 1)
                hi_of(0, k)

            def head(hd):
                first = isinstance(hd, int) and hd == 0
                act.wait_ge(unit_done["A"], hd + 1)
                if not first:
                    act.wait_ge(u_made, hd)
                A(rec[:, 2:2 + NC_], ps[:, 0, 0:NC_], ACT.Copy)
                A(rec[:, 2 + LAT:2 + TA], flat(ps[:, 1:3, :]), ACT.Copy).then_inc(rec_evac, 1)
                round_hi("A", hd + 1)
                act.wait_ge(unit_done["B"], hd + 1)
                A(Y[:, hd], flat(AB67), ACT.Gelu_apprx_tanh).then_inc(g_made, 1)
                round_hi("B", hd + 1)
                for gi in range(4):
                    d, b = gi // 2, 3 if gi % 2 == 0 else 0
                    dst, name = ((RA[d], "gate_a_b"), (IB[d], "gate_x_b"))[gi % 2]
                    act.wait_ge(gate_done, 4 * hd + gi + 1)
                    if not first:
                        act.wait_ge(scan_done, 2 * hd - 1 + d)
                    A(dst[:, 0:NC_], ps[:, b, 0:NC_], ACT.Sigmoid, bias=col(name, d * NH + hd))
                    A(dst[:, LAT:TA], flat(ps[:, b + 1:b + 3, :]), ACT.Sigmoid, bias=col(name, d * NH + hd))\
                        .then_inc(gate_evac, 1)
                for d in range(2):
                    act.wait_ge(gate_evac, 4 * hd + 2 * d + 2)
                    if not first:
                        act.wait_ge(gy_made, hd)
                    A(TH[d][:], RA[d][:], ACT.Tanh, scale=s_tanh[:, bass.ds(d * NH + hd, 1)])\
                        .then_inc(tanh_made, 1)
                for d in range(2):
                    A(RA[d][:], RA[d][:], ACT.Exp, scale=s_exp[:, bass.ds(d * NH + hd, 1)]).then_inc(exp_made, 1)
                for d in range(2):
                    act.wait_ge(tanh_made, 2 * hd + d + 1)
                    A(TH[d][:], TH[d][:], ACT.Sqrt).then_inc(sqrt_made, 1)

            act.wait_ge(lam_ready, 1)
            act.wait_ge(zeros_ready, 1)
            head(0)
            with act.Fori(1, NH) as hd:
                head(hd)
            for k in range(KT):
                act.wait_ge(gy_made, k + 1)
                hi_of(1, k)
            for m in range(KT):
                s, n = "AB"[m % 2], NH + m // 2
                act.wait_ge(unit_done[s], n + 1)
                if m == 0:
                    act.wait_ge(h_ready, 16)
                A(Y[:, m], flat((AB01, AB23)[m % 2]), ACT.Copy).then_inc(y_evac, 1)
                act.wait_ge(y_evac, m + 1)
                square(1, m, Y[:, m])
                round_hi(s, n + 1)
            round_hi("C", 0)
            norm_root(1)

            def before_ffn(L):
                q = 2 + 4 * L
                for m in range(KT):
                    act.wait_ge(x_new, 8 * (2 * L) + m + 1)
                    square(q, m, X[:, m])
                norm_root(q)
                act.wait_ge(coef_ready, 2 + L)
                for k in range(KT):
                    affine(1 + 2 * L, k, Y[:, k], L, 1)
                    act.wait_ge(affine_made, 8 * (1 + 2 * L) + k + 1)
                    hi_of(2 + 2 * L, k)

            def ffn_step(L, j):
                n, c = N_FFN[L] + j, FJ * L + j
                static = isinstance(j, int)
                last = static and n + 1 == N_AB
                act.wait_ge(unit_done["A"], n + 1)
                if not (static and c == 0):
                    act.wait_ge(conv_done, c)
                A(Ub[:, 1:T + 1], flat(AB01), ACT.Copy).then_inc(u_evac, 1)
                act.wait_ge(u_evac, c + 1)
                if not (static and c == 0):
                    act.wait_ge(f_mul, c)
                A(S[0][:], Ub[:, 1:T + 1], ACT.Identity, scale=col("ffn_conv_w", 72 * L + 24 + j),
                  bias=col("ffn_conv_b", 24 * L + j)).then_inc(tap_done, 1)
                if not last:
                    round_hi("A", n + 1)
                act.wait_ge(conv_done, c + 1)
                A(S[0][:], S[0][:], ACT.Gelu_apprx_tanh).then_inc(gelu_done, 1)
                if not (static and c == 0):
                    round_hi("C", c)
                act.wait_ge(f_mul, c + 1)
                A(F_hi[:], S[1][:], ACT.Copy).then_inc(f_hi, 1)
                if not last:
                    round_hi("B", n + 1)

            def after_ffn(L):
                for m in range(KT):
                    act.wait_ge(d_added, 8 * (FJ * (L + 1) - 1) + m + 1)
                    square(3 + 4 * L, m, Y[:, m])
                norm_root(3 + 4 * L)

            def ffn(L):
                ffn_step(L, 0)
                with act.Fori(1, FJ - 1) as j:
                    ffn_step(L, j)
                ffn_step(L, FJ - 1)
                after_ffn(L)

            before_ffn(0)
            ffn(0)
            for m in range(KT):
                act.wait_ge(x_new, 8 * 1 + m + 1)
                square(4, m, X[:, m])
            norm_root(4)
            act.wait_ge(coef_ready, 3)
            act.wait_ge(pads_ready, 1)
            for k in range(KT):
                affine(2, k, Y[:, k], 1, 0)
                act.wait_ge(affine_made, 16 + k + 1)
                if k:
                    act.wait_ge(diff_made, k)
                A(col_x[:, :, 8:8 + GW], Y[:, k].rearrange("p (r c) -> p r c", c=GW), ACT.Copy)\
                    .then_inc(col_loaded, 1)
                if k:
                    hi_of(3, k - 1)
            act.wait_ge(diff_made, KT)
            hi_of(3, KT - 1)
            for mt in range(KT):
                if mt % 4 == 3:
                    act.wait_ge(unit_done["AB"[mt // 4]], N_POOL + 1)
                else:
                    act.wait_ge(pool_mm, mt + 1 - mt // 4)
                A(Y[:, mt], flat((AB01, AB23)[mt % 2]), ACT.Identity, scale=col("pool_scale", mt),
                  bias=pbs[:, mt:mt + 1]).then_inc(y_evac, 1)
                act.wait_ge(y_evac, 8 + mt + 1)
                square(5, mt, Y[:, mt])
            round_hi("A", N_FFN[1])
            round_hi("B", N_FFN[1])
            norm_root(5)
            before_ffn(1)
            ffn(1)

        @block.gpsimd
        def _(pool):
            TT = pool.tensor_tensor

            def lo_of_unit(s, n):
                pool.wait_ge(w_hi[s], n + 1)
                TT(W_lo[s][:], raw[s][:], W_hi[s][:].bitcast(F32), ALU.subtract).then_inc(w_ready[s], 1)

            def lo_of_tile(fill, k):
                pool.wait_ge(h_hi, 8 * fill + k + 1)
                TT(H_lo[:, k], Y[:, k], H_hi[:, k].bitcast(F32), ALU.subtract).then_inc(h_ready, 1)

            def odd_sums(q):
                for m in range(3, KT, 2):
                    pool.wait_ge(sq_made, 8 * q + m + 1)
                    if m > 3:
                        pool.wait_ge(sum_odd, 3 * q + m // 2 - 1)
                    TT(acc[1][:], acc[1][:], S[1][:], ALU.add).then_inc(sum_odd, 1)

            pool.memset(ones[:], 1.0).then_inc(memset_done, 1)
            pool.memset(eps[:], EPS).then_inc(memset_done, 1)
            pool.memset(s_exp[:], 0.0).then_inc(memset_done, 1)
            odd_sums(0)
            lo_of_unit("A", 0)
            lo_of_unit("B", 0)
            pool.wait_ge(chi, 1)
            TT(Hc_lo[:], ctx_x[:], Hc_hi[:].bitcast(F32), ALU.subtract).then_inc(hc_ready, 1)
            pool.wait_ge(hc_ready, 1)
            pool.wait_ge(rb_done, 1)
            for t in (rec[:, 0:2], rec[:, 2 + NC_:2 + LAT], rec[:, 2 + TA:3 + TA],
                      *(b[:, NC_:LAT] for b in (*RA, *IB))):
                ms = pool.memset(t, 0.0)
            ms.then_inc(zeros_ready, 1)
            for k in range(KT):
                lo_of_tile(0, k)

            def head(hd):
                lo_of_unit("A", hd + 1)
                lo_of_unit("B", hd + 1)
                pool.wait_ge(u_made, hd + 1)
                for d in range(2):
                    pool.wait_ge(gate_evac, 4 * hd + 2 * d + 2)
                    TT(IB[d][:], IB[d][:], u[:], ALU.mult).then_inc(iu_made, 1)

            head(0)
            with pool.Fori(1, NH) as hd:
                head(hd)
            for k in range(KT):
                lo_of_tile(1, k)
            for m in range(KT):
                lo_of_unit("AB"[m % 2], NH + m // 2 + 1)
                if m in (3, 5, 7):
                    pool.wait_ge(sq_made, 8 + m + 1)
                    if m > 3:
                        pool.wait_ge(sum_odd, 3 + m // 2 - 1)
                    TT(acc[1][:], acc[1][:], S[1][:], ALU.add).then_inc(sum_odd, 1)
            lo_of_unit("C", 0)

            def before_ffn(L):
                odd_sums(2 + 4 * L)
                pool.memset(Ub[:, 0:1], 0.0)
                pool.memset(Ub[:, T + 1:T + 2], 0.0)
                for k in range(KT):
                    lo_of_tile(2 + 2 * L, k)
                    pool.wait_ge(h_ready, 8 * (2 + 2 * L) + k + 1)
                    pool.memset(Y[:, k], 0.0).then_inc(y_zero, 1)

            def ffn_step(L, j):
                n, c = N_FFN[L] + j, FJ * L + j
                static = isinstance(j, int)
                last = static and n + 1 == N_AB
                if not last:
                    lo_of_unit("A", n + 1)
                if not (static and c == 0):
                    lo_of_unit("C", c)
                pool.wait_ge(f_hi, c + 1)
                TT(F_lo[:], S[1][:], F_hi[:].bitcast(F32), ALU.subtract).then_inc(f_ready, 1)
                if not last:
                    lo_of_unit("B", n + 1)

            def ffn(L):
                ffn_step(L, 0)
                with pool.Fori(1, FJ - 1) as j:
                    ffn_step(L, j)
                ffn_step(L, FJ - 1)
                odd_sums(3 + 4 * L)

            before_ffn(0)
            ffn(0)
            odd_sums(4)
            pool.wait_ge(rb_done, 5)
            pool.memset(col_x[:], 0.0)
            pool.memset(row_x[:], 0.0).then_inc(pads_ready, 1)
            for k in range(KT):
                lo_of_tile(3, k)
            odd_sums(5)
            lo_of_unit("A", N_FFN[1])
            lo_of_unit("B", N_FFN[1])
            before_ffn(1)
            ffn(1)

        @block.vector
        def _(dve):
            TT, STT, TS = dve.tensor_tensor, dve.scalar_tensor_tensor, dve.tensor_scalar

            def even_sums(q):
                for m in range(2, KT, 2):
                    dve.wait_ge(sq_made, 8 * q + m + 1)
                    if m > 2:
                        dve.wait_ge(sum_even, 3 * q + m // 2 - 1)
                    TT(acc[0][:], acc[0][:], S[0][:], ALU.add).then_inc(sum_even, 1)

            def norm_diagonal(q):
                dve.wait_ge(rms_made, q + 1)
                dve.reciprocal(rstd[:], rms[:]).then_inc(rstd_made, 1)
                dve.wait_ge(rstd_made, q + 1)
                if q:
                    dve.wait_ge(rb_done, q)
                TT(diag[:], ident[:].unsqueeze(1).to_broadcast([P, KT, P]),
                   rstd[:].unsqueeze(2).to_broadcast([P, KT, P]), ALU.mult).then_inc(diag_made, 1)

            def add_ada_bias(out, unit0, group):
                dve.wait_ge(ada_out, 4 + group)
                TT(M[:, bass.ds(unit0, 2)], out, col("ada_b", unit0, 2), ALU.add).then_inc(ada_added, 1)

            def coefs(i, L, ffn_part):
                a, o = 48 * L + 24 * ffn_part, 8 * L
                STT(cA[:, i], M[:, a + 8:a + 16], 1.0,
                    col(("npre_mix", "npre_ffn")[ffn_part], o, 8), ALU.add, ALU.mult)

            def gates(i, L, ffn_part):
                a, o = 48 * L + 24 * ffn_part, 8 * L
                return TT(cG[:, i], M[:, a + 16:a + 24], col(("npost_mix", "npost_ffn")[ffn_part], o, 8), ALU.mult)

            def scale_tiles(i, q, src):
                dve.wait_ge(rb_done, q + 1)
                for k in range(KT):
                    TT(Y[:, k], src[:, k], flat(AB67), ALU.mult).then_inc(x_scaled, 1)

            def add_residual(i, q):
                dve.wait_ge(rb_done, q + 1)
                for m in range(KT + 1):
                    if m < KT:
                        STT(Y[:, m], Y[:, m], cG[:, i, m:m + 1], flat(AB67), ALU.mult, ALU.mult)\
                            .then_inc(y_scaled, 1)
                    if m:
                        if i == 0 and m % 2:
                            dve.wait_ge(res_full[m // 2], 16)
                        dve.wait_ge(y_scaled, 8 * i + m)
                        TT(X[:, m - 1], X[:, m - 1], Y[:, m - 1], ALU.add).then_inc(x_new, 1)

            dve.wait_ge(softplus_step, 2)
            TS(sp[:, 2], sp[:, 1], 1.0, None, ALU.add).then_inc(softplus_step, 1)
            dve.wait_ge(softplus_step, 4)
            TS(sp[:, 4], sp[:, 2], -1.0, None, ALU.add).then_inc(softplus_step, 1)
            dve.wait_ge(softplus_step, 5)
            TS(sp[:, 5], sp[:, 4], 0.0, None, ALU.is_equal).then_inc(softplus_step, 1)
            dve.wait_ge(softplus_step, 6)
            TT(sp[:, 3], sp[:, 3], sp[:, 5], ALU.add).then_inc(softplus_step, 1)
            TT(sp[:, 4], sp[:, 4], sp[:, 5], ALU.add).then_inc(softplus_step, 1)
            dve.wait_ge(softplus_step, 8)
            dve.reciprocal(sp[:, 6], sp[:, 4]).then_inc(softplus_step, 1)
            TT(sp[:, 3], sp[:, 3], sp[:, 1], ALU.mult).then_inc(softplus_step, 1)
            dve.wait_ge(softplus_step, 10)
            TT(sp[:, 3], sp[:, 3], sp[:, 6], ALU.mult).then_inc(softplus_step, 1)
            TS(sp[:, 7], col("lam", 0, 16), -1.0, 0.0, ALU.mult, ALU.max).then_inc(softplus_step, 1)
            dve.wait_ge(softplus_step, 12)
            TT(sp[:, 3], sp[:, 3], sp[:, 7], ALU.add).then_inc(softplus_step, 1)
            dve.wait_ge(softplus_step, 13)
            dve.wait_ge(memset_done, 3)
            TS(s_tanh[:], sp[:, 3], 0.5 * RG_C, None, ALU.mult)
            TS(s_exp[:], sp[:, 3], -RG_C, None, ALU.mult).then_inc(lam_ready, 1)
            TT(pbs[:], col("pool_b", 0, 8), col("pool_scale", 0, 8), ALU.mult)
            even_sums(0)
            dve.wait_ge(const_full, 16)
            norm_diagonal(0)
            dve.wait_ge(crms_made, 1)
            dve.reciprocal(rstd_c[:], rms_c[:]).then_inc(crstd_made, 1)
            dve.wait_ge(crstd_made, 1)
            TT(diag_c[:], ident[:].unsqueeze(1).to_broadcast([P, 2, P]),
               rstd_c[:].unsqueeze(2).to_broadcast([P, 2, P]), ALU.mult).then_inc(cdiag_made, 1)
            dve.wait_ge(crb_done, 1)
            TT(ctx_x[:], ctx_x[:], ps[:, 3, 0:NC_].unsqueeze(1).to_broadcast([P, KT, NC_]), ALU.mult)\
                .then_inc(cscaled, 1)
            dve.wait_ge(ada_out, 4)
            first = ps[:, 2, 0:2 * ADA0].rearrange("p (m v) -> p m v", v=2)
            TT(M[:, 0:ADA0], first[:, :, 0], col("ada_b", 0, ADA0), ALU.add)
            TT(Mc[:], first[:, :, 1], col("ada_b", 0, ADA0), ALU.add).then_inc(ada_added, 1)
            dve.wait_ge(ada_added, 1)
            coefs(0, 0, 0)
            STT(cAc[:], Mc[:, 8:16], 1.0, col("npre_mix", 0, 8), ALU.add, ALU.mult).then_inc(coef_ready, 1)
            scale_tiles(0, 0, Y)

            def convolve(hd):
                dve.wait_ge(rec_evac, hd + 1)
                if not (isinstance(hd, int) and hd == 0):
                    dve.wait_ge(gate_done, 4 * hd)
                    dve.wait_ge(iu_made, 2 * hd)
                TS(u[:], rec[:, 0:TA], col("rg_conv_w", hd), col("rg_conv_b", hd), ALU.mult, ALU.add)\
                    .then_inc(conv_step, 1)
                for tap in range(1, 4):
                    dve.wait_ge(conv_step, 3 * hd + tap)
                    STT(u[:], rec[:, tap:tap + TA], col("rg_conv_w", tap * NH + hd), u[:], ALU.mult, ALU.add)\
                        .then_inc(conv_step if tap < 3 else u_made, 1)

            def scans(hd, d):
                n = 2 * hd + d + 1
                dve.wait_ge(sqrt_made, n)
                STT(TH[d][:], RA[d][:], 1.0, TH[d][:], ALU.add, ALU.mult).then_inc(mult_made, 1)
                dve.wait_ge(mult_made, n)
                dve.wait_ge(iu_made, n)
                TT(IB[d][:], IB[d][:], TH[d][:], ALU.mult).then_inc(b_made, 1)
                dve.wait_ge(b_made, n)
                rev = slice(None, None, -1 if d else 1)
                a, b, h = ([t[:, 0:NC_][:, rev], t[:, LAT:TA][:, rev]] for t in (RA[d], IB[d], TH[d]))
                dve.tensor_tensor_scan(h[0], a[0], b[0], 0.0, ALU.mult, ALU.add).then_inc(scan_ctx, 1)
                dve.wait_ge(scan_ctx, n)
                dve.tensor_tensor_scan(h[1], a[1], b[1], h[0][:, NC_ - 1:NC_], ALU.mult, ALU.add)\
                    .then_inc(scan_done, 1)

            def combine(hd):
                dve.wait_ge(scan_done, 2 * hd + 2)
                TT(TH[0][:, LAT:TA], TH[0][:, LAT:TA], TH[1][:, LAT:TA], ALU.add).then_inc(ysum_made, 1)
                dve.wait_ge(ysum_made, hd + 1)
                dve.wait_ge(g_made, hd + 1)
                TT(Y[:, hd], Y[:, hd], TH[0][:, LAT:TA], ALU.mult).then_inc(gy_made, 1)

            def ada_first(hd):
                add_ada_bias(ps[:, 3, 0:2], ADA0 + 4 * hd, 2 * hd + 1)

            def ada_second(hd):
                add_ada_bias(ps[:, 6, 0:2], ADA0 + 4 * hd + 2, 2 * hd + 2)

            def head(hd):
                scans(hd, 0)
                ada_first(hd + 1)
                convolve(hd + 1)
                scans(hd, 1)
                combine(hd)
                ada_second(hd + 1)

            dve.wait_ge(zeros_ready, 1)
            ada_first(0)
            convolve(0)
            ada_second(0)
            head(0)
            with dve.Fori(1, NH - 1) as hd:
                head(hd)
            for d in range(2):
                scans(NH - 1, d)
            combine(NH - 1)
            dve.wait_ge(ada_added, 2 * NH + 1)
            coefs(1, 0, 1)
            gates(0, 0, 0)
            gates(1, 0, 1).then_inc(coef_ready, 1)
            even_sums(1)
            norm_diagonal(1)
            dve.wait_ge(coef_ready, 2)
            add_residual(0, 1)

            def before_ffn(L):
                q = 2 + 4 * L
                even_sums(q)
                norm_diagonal(q)
                scale_tiles(1 + 2 * L, q, X)

            def ffn_step(L, j):
                n, c = N_FFN[L] + j, FJ * L + j
                at0 = isinstance(j, int) and j == 0
                if not at0:
                    add_down(L, j - 1)
                dve.wait_ge(tap_done, c + 1)
                STT(S[0][:], Ub[:, 0:T], col("ffn_conv_w", 72 * L + j), S[0][:], ALU.mult, ALU.add)\
                    .then_inc(conv_a, 1)
                dve.wait_ge(conv_a, c + 1)
                STT(S[0][:], Ub[:, 2:T + 2], col("ffn_conv_w", 72 * L + 48 + j), S[0][:], ALU.mult, ALU.add)\
                    .then_inc(conv_done, 1)
                if L == 0 and not at0:
                    add_ada_bias(ps[:, 0, 0:2], 48 + 2 * j, 2 * NH + 1 + j)
                dve.wait_ge(gelu_done, c + 1)
                dve.wait_ge(unit_done["B"], n + 1)
                if not (isinstance(c, int) and c == 0):
                    dve.wait_ge(f_ready, c)
                TT(S[1][:], S[0][:], flat(AB23), ALU.mult).then_inc(f_mul, 1)
                if L == 0 and at0:
                    add_ada_bias(ps[:, 0, 0:2], 48, 2 * NH + 1)

            def add_down(L, j):
                for m in range(KT):
                    dve.wait_ge(d_done, 8 * (FJ * L + j) + m + 1)
                    b = 4 + 2 * (m % 2)
                    TT(Y[:, m], Y[:, m], flat(ps[:, b:b + 2, :]), ALU.add).then_inc(d_added, 1)

            def ffn(L):
                ffn_step(L, 0)
                dve.wait_ge(y_zero, 8 * (L + 1))
                with dve.Fori(1, FJ - 1) as j:
                    ffn_step(L, j)
                ffn_step(L, FJ - 1)
                add_down(L, FJ - 1)
                even_sums(3 + 4 * L)
                norm_diagonal(3 + 4 * L)

            before_ffn(0)
            ffn(0)
            dve.wait_ge(ada_added, 2 * NH + 1 + FJ)
            coefs(2, 1, 0)
            coefs(3, 1, 1)
            gates(2, 1, 0)
            gates(3, 1, 1).then_inc(coef_ready, 1)
            add_residual(1, 3)
            even_sums(4)
            norm_diagonal(4)
            scale_tiles(2, 4, X)

            steps = [0]

            def step(out, a, b, op=ALU.add):
                if steps[0]:
                    dve.wait_ge(pool_step, steps[0])
                TT(out, a, b, op).then_inc(pool_step, 1)
                steps[0] += 1

            for k in range(KT):
                w = WINDOWS[k // 2]
                dve.wait_ge(col_loaded, k + 1)
                src, s = col_x, 2
                while s <= w:
                    lo, hi = 8 - (w - s) // 2, 8 + GW + (w - s) // 2
                    src_ap = src if s == 2 else src_v
                    if s == w:
                        dst = row_x[:, 8:8 + GR, :]
                    else:
                        dst_v = pt[(s.bit_length()) % 2][:, 0:GR * (GW + 16)].rearrange("p (r c) -> p r c", c=GW + 16)
                        dst = dst_v[:, :, lo:hi]
                    left, right = (1, 0) if s == 2 else (s // 4, -(s // 4))
                    step(dst, src_ap[:, :, lo - left:hi - left], src_ap[:, :, lo - right:hi - right])
                    if s < w:
                        src_v = dst_v
                    s *= 2
                s, cur = 2, row_x[:].rearrange("p r c -> p (r c)")
                while s <= w:
                    lo, hi = 8 - (w - s) // 2, 8 + GR + (w - s) // 2
                    dst = pt[s.bit_length() % 2]
                    left, right = (1, 0) if s == 2 else (s // 4, -(s // 4))
                    step(dst[:, lo * GW:hi * GW], cur[:, (lo - left) * GW:(hi - left) * GW],
                         cur[:, (lo - right) * GW:(hi - right) * GW])
                    cur = dst
                    s *= 2
                own = cur[:, 8 * GW:(8 + GR) * GW]
                if k % 2 == 0:
                    dve.wait_ge(cnt_full[(k // 2) % 2], 16 * (k // 4 + 1))
                step(own, own, S[(k // 2) % 2][:], ALU.mult)
                dve.wait_ge(pool_step, steps[0])
                TT(Y[:, k], own, Y[:, k], ALU.subtract).then_inc(diff_made, 1)
            even_sums(5)
            norm_diagonal(5)
            add_residual(2, 5)
            before_ffn(1)
            ffn(1)
            add_residual(3, 7)


def kernel(**inputs):
    import numpy as np
    import concourse.bacc as bacc
    from concourse.bass_utils import run_bass_kernel_spmd as run

    a = {k: np.asarray(v) for k, v in inputs.items()}

    def channel_major(x):
        return np.ascontiguousarray(x.reshape(x.shape[0], -1, P).transpose(2, 1, 0))

    def columns(v):
        return v.reshape(-1, P).T

    def out_tiles(w):
        return w.reshape(KT, P, -1, P).transpose(2, 1, 0, 3).reshape(-1, P, D)

    par = np.concatenate([columns(a[n]) for n in (
        "ada_b", "norm_pre_mix", "norm_post_mix", "norm_pre_ffn", "norm_post_ffn", "rg_conv_w", "rg_conv_b",
        "rg_gate_a_b", "rg_gate_x_b", "rg_lambda", "pool_b", "pool_scale", "ffn_conv_w", "ffn_conv_b")]
        + [np.stack([columns(a["c"]), columns(a["c_ctx"])], axis=-1).reshape(P, 16)], axis=1)
    w_in, w_out = out_tiles(a["rg_w_in"][0]), out_tiles(a["rg_w_out"][0])
    up = [out_tiles(a["ffn_w_up"][i]) for i in range(2)]
    down = a["ffn_w_down"].reshape(2 * FJ, P, D)
    pool = a["pool_w"][0].reshape(2, 2, 2, P, 256).transpose(0, 3, 1, 2, 4).reshape(2, P, D)
    slot_a = np.concatenate([w_in[NH:], w_out[0::2], up[0][:FJ], pool[0:1], up[1][:FJ]])
    slot_b = np.concatenate([w_in[:NH], w_out[1::2], up[0][FJ:], pool[1:2], up[1][FJ:]])
    gw = np.stack([a["rg_gate_a_w"][0], a["rg_gate_x_w"][0]], axis=1)
    gw = gw.transpose(2, 3, 0, 1, 4).reshape(NH, P, 4, P)
    ada = np.concatenate([out_tiles(a["ada_w"][i]) for i in range(2)])

    def reach(n, w):
        t = np.arange(n)
        return np.clip(t + w // 2, 0, n) - np.clip(t - w // 2, 0, n)

    cnt = np.stack([(1.0 / np.outer(reach(GR, w), reach(GW, w))).reshape(T) for w in WINDOWS]).astype(np.float32)
    arrays = {
        "xT": channel_major(a["x"][0]), "ctxT": channel_major(a["ctx"][0]), "params": par, "ada": ada,
        "wA": slot_a, "wB": slot_b, "wC": down, "gatew": gw, "poolcnt": cnt,
        "ident_in": np.eye(P, dtype=np.float32),
    }
    arrays = {k: np.ascontiguousarray(v) for k, v in arrays.items()}
    nc = bacc.Bacc("TRN2", target_bir_lowering=False, num_devices=1, dynamic_dma_scratch_size=1024)
    aps = [nc.dram_tensor(k, v.shape, F32, kind="ExternalInput").ap() for k, v in arrays.items()]
    out = nc.dram_tensor("outT", (P, KT, T), F32, kind="ExternalOutput").ap()
    build_trunk(nc, *aps, out)
    r = run(nc, [arrays], core_ids=[0])
    return r.results[0]["outT"].transpose(2, 1, 0).reshape(1, T, D)
```

```python
from contextlib import ExitStack

import concourse.bass as bass
from concourse import mybir

P = 128
D = 1024
T = 1024
NC_ = 256
KT = D // P
HF = 512
NH = 8
FJ = 3 * D // P
GW = 64
GR = T // GW
WINDOWS = (2, 4, 8, 16)
EPS = 1e-6
RG_C = 8.0

LAT = NC_ + 2
TA = LAT + T

_COLS = {}
_at = 0
for _name, _n in (("ada_b", 96), ("npre_mix", 16), ("npost_mix", 16), ("npre_ffn", 16), ("npost_ffn", 16),
                  ("rg_conv_w", 32), ("rg_conv_b", 8), ("gate_a_b", 16), ("gate_x_b", 16), ("lam", 16),
                  ("pool_b", 8), ("pool_scale", 8), ("ffn_conv_w", 144), ("ffn_conv_b", 48), ("cond", 16)):
    _COLS[_name] = _at
    _at += _n
NPAR = _at

ADA0 = 16
N_WOUT = NH
N_FFN = (NH + 4, NH + 4 + FJ + 1)
N_POOL = NH + 4 + FJ
N_AB = N_FFN[1] + FJ

F32 = mybir.dt.float32
F32R = mybir.dt.float32r
ALU = mybir.AluOpType
ACT = mybir.ActivationFunctionType


def build_trunk(nc, xT, ctxT, params, ada, wA, wB, wC, gatew, poolcnt, ident_in, outT):
    with ExitStack() as top:
        def sb(name, shape, dt=F32, scope=top):
            return scope.enter_context(nc.sbuf_tensor(name, shape, dt))

        def sem(name):
            return top.enter_context(nc.semaphore(name))

        Y = sb("Y", [P, KT, T])
        slots = ("A", "B", "C")
        raw = {s: sb(f"raw{s}", [P, D]) for s in slots}
        W_hi = {s: sb(f"W{s}_hi", [P, D], F32R) for s in slots}
        W_lo = {s: sb(f"W{s}_lo", [P, D], F32R) for s in slots}
        S = [sb(f"S{i}", [P, T]) for i in range(2)]
        par = sb("par", [P, NPAR])
        M = sb("M", [P, 96])
        Mc = sb("Mc", [P, ADA0])
        silu_c = sb("silu_c", [P, KT, 2])
        cA = sb("cA", [P, 4, KT])
        cAc = sb("cAc", [P, KT])
        cG = sb("cG", [P, 4, KT])
        pbs = sb("pbs", [P, KT])
        ident = sb("ident", [P, P])
        ones = sb("ones", [P, P])
        eps = sb("eps", [P, 1])
        rms = sb("rms", [P, KT])
        rstd = sb("rstd", [P, KT])
        rms_c = sb("rms_c", [P, 2])
        rstd_c = sb("rstd_c", [P, 2])
        sp = sb("sp", [P, 8, 2 * NH])
        s_tanh = sb("s_tanh", [P, 2 * NH])
        s_exp = sb("s_exp", [P, 2 * NH])

        def overlay(*plan):
            with ExitStack() as scope:
                out = []
                for n, item in enumerate(plan):
                    if isinstance(item, tuple):
                        out.append(sb(*item, scope=scope))
                    else:
                        sb(f"gap_{plan[-1][0]}_{n}", [P, int(item * 256)], scope=scope)
            return out

        H_hi, H_lo = overlay(("H_hi", [P, KT, T], F32R), ("H_lo", [P, KT, T], F32R))
        ada_first, ctx_x, ctx_sq, diag_c = overlay(
            ("ada_first", [P, ADA0, D]), ("ctx_x", [P, KT, NC_]), ("ctx_sq", [P, KT, NC_]), ("diag_c", [P, 2, P]))
        rec, u, RA0, Hc_hi, Hc_lo, RA1, IB0, IB1, TH0, TH1, gw = overlay(
            64, ("rec", [P, TA + 3]), ("u", [P, TA]), ("RA0", [P, TA]), 1.25,
            ("Hc_hi", [P, KT, NC_], F32R), ("Hc_lo", [P, KT, NC_], F32R), ("RA1", [P, TA]),
            ("IB0", [P, TA]), ("IB1", [P, TA]), ("TH0", [P, TA]), ("TH1", [P, TA]), ("gw", [P, 4, P]))
        RA, IB, TH = (RA0, RA1), (IB0, IB1), (TH0, TH1)
        E0, E1, red = overlay(
            124, ("E0", [P, KT, P]), ("E1", [P, KT, P]), ("red", [P, 4, P]))
        E = (E0, E1)
        X, Ub, acc0, acc1, diag, F_hi, F_lo = overlay(
            64, ("X", [P, KT, T]), ("Ub", [P, T + 2]), ("acc0", [P, T]), ("acc1", [P, T]),
            ("diag", [P, KT, P]), ("F_hi", [P, T], F32R), ("F_lo", [P, T], F32R))
        acc = (acc0, acc1)
        col_v, row_v, pt0, pt1, col_p, row_p, pt_p = overlay(
            96, ("col_v", [P, GR, GW + 16]), ("row_v", [P, GR + 16, GW]),
            ("pt0", [P, (GR + 14) * GW]), ("pt1", [P, (GR + 14) * GW]),
            ("col_p", [P, GR, GW + 4]), ("row_p", [P, GR + 4, GW]), ("pt_p", [P, (GR + 3) * GW]))
        ps = top.enter_context(nc.psum_tensor("ps", [P, 8, 512], F32))
        AB01, AB23, AB45, AB67 = (ps[:, b:b + 2, :] for b in (0, 2, 4, 6))

        par_full, ctx_full, const_full = sem("par_full"), sem("ctx_full"), sem("const_full")
        x_full = [sem(f"x_full{q}") for q in range(4)]
        res_full = [sem(f"res_full{q}") for q in range(4)]
        ada_first_full = [sem(f"ada_first_full{q}") for q in range(4)]
        e_full = [sem(f"ada_full{i}") for i in range(2)]
        raw_full = {s: sem(f"raw_full_{s}") for s in slots}
        w_hi = {s: sem(f"w_hi_{s}") for s in slots}
        w_ready = {s: sem(f"w_ready_{s}") for s in slots}
        unit_done = {s: sem(f"unit_done_{s}") for s in "AB"}
        gw_full, gate_done, gate_evac = sem("gw_full"), sem("gate_done"), sem("gate_evac")
        memset_done, zeros_ready = sem("memset_done"), sem("zeros_ready")
        silu_done, softplus_step, lam_ready = sem("silu_done"), sem("softplus_step"), sem("lam_ready")
        e_mul, red_made = sem("ada_mul"), sem("ada_red_made")
        ada_out, ada_added, coef_ready = sem("ada_out"), sem("ada_added"), sem("coef_ready")
        sq_made, sum_even, sum_odd = sem("sq_made"), sem("sum_even"), sem("sum_odd")
        ssq_done, rms_made, rstd_made = sem("ssq_done"), sem("rms_made"), sem("rstd_made")
        diag_made, rb_done = sem("diag_made"), sem("rb_done")
        csq_made, cssq_done, crms_made = sem("ctx_sq_made"), sem("ctx_ssq_done"), sem("ctx_rms_made")
        crstd_made, cdiag_made, crb_done = sem("ctx_rstd_made"), sem("ctx_diag_made"), sem("ctx_rb_done")
        cscaled, caffine, chi, hc_ready = sem("ctx_scaled"), sem("ctx_affine"), sem("ctx_hi"), sem("ctx_h_ready")
        x_scaled, affine_made, h_hi = sem("x_scaled"), sem("affine_made"), sem("h_hi")
        h_ready = (sem("h_ready_even"), sem("h_ready_odd"))
        y_scaled, y_evac = sem("y_scaled"), sem("y_evac")
        x_new = (sem("x_new_even"), sem("x_new_odd"))
        rec_evac, conv_step, u_made = sem("rec_evac"), sem("conv_step"), sem("u_made")
        g_made, tanh_made, exp_made, sqrt_made = sem("g_made"), sem("tanh_made"), sem("exp_made"), sem("sqrt_made")
        mult_made, iu_made, b_made = sem("mult_made"), sem("iu_made"), sem("b_made")
        scan_ctx, scan_done, ysum_made, gy_made = sem("scan_ctx"), sem("scan_done"), sem("ysum_made"), sem("gy_made")
        u_evac, tap_done, conv_a, conv_done = sem("u_evac"), sem("tap_done"), sem("conv_a"), sem("conv_done")
        gelu_done, f_mul, f_hi, f_ready = sem("gelu_done"), sem("f_mul"), sem("f_hi"), sem("f_ready")
        d_done, d_added = sem("d_done"), sem("d_added")
        pads_ready, tile_affine = sem("pads_ready"), sem("tile_affine")
        col_loaded = {e: sem(f"col_loaded_{e}") for e in "vp"}
        pool_step = {e: sem(f"pool_step_{e}") for e in "vp"}
        diff_made = {e: sem(f"diff_made_{e}") for e in "vp"}
        diff_hi, diff_ready = {e: sem(f"diff_hi_{e}") for e in "vp"}, {e: sem(f"diff_ready_{e}") for e in "vp"}
        cnt_full = {e: sem(f"cnt_full_{e}") for e in "vp"}
        pool_mm, out_done = sem("pool_mm"), sem("out_done")

        block = top.enter_context(nc.Block())

        def col(name, n=0, w=1):
            c = _COLS[name] + n
            return par[:, bass.ds(c, w)]

        def flat(banks):
            return banks.rearrange("p a b -> p (a b)")

        def hs(h):
            return slice(h * HF, h * HF + HF)

        H_BASE = {0: 0, 1: 16, 2: 24, 4: 40}
        FILL = {0: 0, 1: 2, 3: 4}
        AFFINE_BASE = {0: 0, 1: 8, 3: 16}
        POOL_TILES = {"p": (0, 1, 2, 3), "v": (4, 5, 6, 7)}
        POOL_GROUPS = (0, 2, 3, 1)
        POOL_OUT = tuple(2 * g + m for g in POOL_GROUPS for m in range(2))

        def tiles_of(q):
            return POOL_OUT if q == 5 else tuple(range(KT))

        def ssq_bank(q, h):
            return (0 if q in (3, 7) else 4) + h

        def rb_bank(q, h):
            return (2 if q in (3, 7) else 6) + h

        def wait_h(eng, fill, h, k):
            eng.wait_ge(h_ready[k % 2], H_BASE[fill] // 2 + 4 * h + k // 2 + 1)

        def window_stages(w):
            return w.bit_length() - 1

        def pool_steps(e, t):
            return sum(2 * window_stages(WINDOWS[k // 2]) + 1 for k in POOL_TILES[e][:t])

        def wait_new(eng, i, h, m):
            eng.wait_ge(x_new[m % 2], 8 * i + 4 * h + m // 2 + 1)

        @block.sync
        def _(sp_):
            def load_raw(s, n):
                if not (isinstance(n, int) and n == 0):
                    sp_.wait_ge(w_ready[s], n)
                sp_.dma_start(raw[s][:], {"A": wA, "B": wB, "C": wC}[s][n]).then_inc(raw_full[s], 16)

            def load_pair(p):
                if not (isinstance(p, int) and p == 0):
                    sp_.wait_ge(red_made, 2 * p)
                for i in range(2):
                    sp_.dma_start(E[i][:], ada[ADA0 + 2 * p + i].rearrange("p (k m) -> p k m", k=KT))\
                       .then_inc(e_full[i], 16)

            def load_first(q):
                sp_.dma_start(ada_first[:, 4 * q:4 * q + 4], ada[4 * q:4 * q + 4].rearrange("u p c -> p u c"))\
                   .then_inc(ada_first_full[q], 16)

            def load_x(q, dst, full):
                sp_.dma_start(dst[:, 2 * q:2 * q + 2], xT[:, 2 * q:2 * q + 2]).then_inc(full[q], 16)

            sp_.dma_start(par[:], params).then_inc(par_full, 16)
            load_first(0)
            load_x(0, Y, x_full)
            load_x(1, Y, x_full)
            load_first(1)
            load_x(2, Y, x_full)
            load_x(3, Y, x_full)
            sp_.dma_start(ctx_x[:], ctxT).then_inc(ctx_full, 16)
            sp_.dma_start(ident[:], ident_in).then_inc(const_full, 16)
            load_first(2)
            load_first(3)
            load_raw("A", 0)
            load_raw("B", 0)
            load_pair(0)
            load_raw("A", 1)
            load_raw("B", 1)
            sp_.dma_start(gw[:], gatew[0]).then_inc(gw_full, 16)

            def head_loads(hd, last=False):
                load_raw("A", hd + 2)
                load_pair(2 * hd + 1)
                load_raw("B", hd + 2)
                if not last:
                    sp_.wait_ge(gate_done, 4 * hd + 4)
                    sp_.dma_start(gw[:], gatew[hd + 1]).then_inc(gw_full, 16)
                load_pair(2 * hd + 2)

            head_loads(0)
            with sp_.Fori(1, NH - 1) as hd:
                head_loads(hd)
            head_loads(NH - 1, last=True)
            sp_.wait_ge(gy_made, NH)
            for q in range(4):
                load_x(q, X, res_full)
            load_raw("C", 0)
            for i in range(4):
                load_raw("A", NH + 2 + i)
                load_raw("B", NH + 2 + i)

            def ffn_loads(L, j):
                n, c = N_FFN[L] + j, FJ * L + j
                static = isinstance(j, int)
                if not static or n + 2 < N_AB:
                    load_raw("A", n + 2)
                if L == 0 and not (static and j == FJ - 1):
                    load_pair(2 * NH + j + 1)
                if not static or c + 1 < 2 * FJ:
                    load_raw("C", c + 1)
                if not static or n + 2 < N_AB:
                    load_raw("B", n + 2)

            def ffn(L):
                ffn_loads(L, 0)
                with sp_.Fori(1, FJ - 2) as j:
                    ffn_loads(L, j)
                ffn_loads(L, FJ - 2)
                ffn_loads(L, FJ - 1)

            ffn(0)
            sp_.wait_ge(ssq_done, 10)
            for i, (e, g) in enumerate((("p", 0), ("v", 2), ("p", 1), ("v", 3))):
                if i >= 2:
                    sp_.wait_ge(diff_made[e], 2)
                sp_.dma_start(S["pv".index(e)][:], poolcnt[g:g + 1, :].to_broadcast([P, T]))\
                   .then_inc(cnt_full[e], 16)
            load_raw("A", N_POOL + 2)
            load_raw("B", N_POOL + 2)
            ffn(1)
            for h in range(2):
                for m in range(KT):
                    wait_new(sp_, 3, h, m)
                    sp_.dma_start(outT[:, m, hs(h)], X[:, m, hs(h)]).then_inc(out_done, 16)
            sp_.wait_ge(out_done, 16 * 2 * KT)

        @block.tensor
        def _(pe):
            def product(s, w_cols, pieces, first=True, last=True):
                for w, part in ((W_hi[s], 0), (W_hi[s], 1), (W_lo[s], 0)):
                    for out, hi, lo in pieces:
                        mm = pe.matmul(out, w[:, w_cols:w_cols + P], (hi, lo)[part],
                                       start=first and w is W_hi[s] and part == 0,
                                       stop=last and w is W_lo[s])
                return mm

            def piece(banks, hi, lo, k, h):
                return banks[:, h], hi[:, k, hs(h)], lo[:, k, hs(h)]

            def unit(s, n, banks):
                pe.wait_ge(w_ready[s], n + 1)
                for k in range(KT):
                    mm = product(s, k * P, [piece(banks, H_hi, H_lo, k, h) for h in range(2)], k == 0, k == KT - 1)
                mm.then_inc(unit_done[s], 1)

            def first_units(fill, units, context=None):
                for h in range(2):
                    for s, n, banks in units:
                        pe.wait_ge(w_ready[s], n + 1)
                        for k in range(KT):
                            wait_h(pe, fill, h, k)
                            pieces = [piece(banks, H_hi, H_lo, k, h)]
                            if context is not None and h == 0 and s == "A":
                                pieces.append((context, Hc_hi[:, k], Hc_lo[:, k]))
                            mm = product(s, k * P, pieces, k == 0, k == KT - 1)
                        if h == 1:
                            mm.then_inc(unit_done[s], 1)

            def ada_columns(n_red, n, out):
                pe.wait_ge(red_made, n_red)
                for i in range(n):
                    mm = pe.matmul(out[:, i:i + 1], red[:, i], ones[:, 0:1], start=True, stop=True)
                mm.then_inc(ada_out, 1)

            def square_sums(q, h):
                n = 2 * q + h
                pe.wait_ge(sum_even, 3 * n + 3)
                pe.wait_ge(sum_odd, 3 * n + 3)
                for t in range(4):
                    for a in range(2):
                        c = h * HF + t * P
                        mm = pe.matmul(ps[:, ssq_bank(q, h), t:t + 1], acc[a][:, c:c + P], ones[:, 0:1],
                                       start=a == 0, stop=a == 1)
                mm.then_inc(ssq_done, 1)

            def spread(q, h):
                pe.wait_ge(diag_made, 2 * q + h + 1)
                pe.matmul(ps[:, rb_bank(q, h)], ones[:], diag[:, 4 * h:4 * h + 4], start=True, stop=True)\
                    .then_inc(rb_done, 1)

            def norms(*qs):
                for q in qs:
                    for h in range(2):
                        square_sums(q, h)
                        spread(q, h)

            pe.wait_ge(silu_done, 1)
            for n in range(ADA0):
                pe.wait_ge(ada_first_full[n // 4], 16)
                for k in range(KT):
                    mm = pe.matmul(ps[:, 2, 2 * n:2 * n + 2], ada_first[:, n, k * P:k * P + P], silu_c[:, k],
                                   start=k == 0, stop=k == KT - 1)
                if n == 7:
                    pe.wait_ge(const_full, 16)
                    pe.wait_ge(memset_done, 3)
                    norms(0)
            mm.then_inc(ada_out, 1)
            pe.wait_ge(csq_made, 1)
            for t in range(2):
                for k in range(KT):
                    mm = pe.matmul(ps[:, 0, t:t + 1], ctx_sq[:, k, t * P:(t + 1) * P], ones[:, 0:1],
                                   start=k == 0, stop=k == KT - 1)
            mm.then_inc(cssq_done, 1)
            pe.wait_ge(cdiag_made, 1)
            pe.matmul(ps[:, 3, 0:NC_], ones[:], diag_c[:], start=True, stop=True).then_inc(crb_done, 1)

            def head(hd, last=False):
                if not (isinstance(hd, int) and hd == 0):
                    pe.wait_ge(gate_evac, 4 * hd - 1)
                    ada_columns(4 * hd, 4, ps[:, 3, 0:4])
                    unit("B", hd, AB67)
                pe.wait_ge(gw_full, 16 * hd + 16)
                pe.wait_ge(u_made, hd + 1)
                for gi in range(4):
                    if gi == 0:
                        pe.wait_ge(ada_added, hd + 1)
                    elif gi == 1:
                        pe.wait_ge(rec_evac, hd + 1)
                    else:
                        pe.wait_ge(gate_evac, 4 * hd + gi - 1)
                    b = 3 if gi % 2 == 0 else 0
                    for out, src in ((ps[:, b, 0:NC_], u[:, 0:NC_]), (ps[:, b + 1], u[:, LAT:LAT + HF]),
                                     (ps[:, b + 2], u[:, LAT + HF:TA])):
                        mm = pe.matmul(out, gw[:, gi], src, start=True, stop=True)
                    mm.then_inc(gate_done, 1)
                if not last:
                    pe.wait_ge(gate_evac, 4 * hd + 4)
                    s, n = "A", hd + 1
                    pe.wait_ge(w_ready[s], n + 1)
                    for k in range(KT):
                        pieces = [piece(ps[:, 1:3, :], H_hi, H_lo, k, h) for h in range(2)]
                        pieces.append((ps[:, 0, 0:NC_], Hc_hi[:, k], Hc_lo[:, k]))
                        mm = product(s, k * P, pieces, k == 0, k == KT - 1)
                    mm.then_inc(unit_done[s], 1)

            pe.wait_ge(hc_ready, 1)
            pe.wait_ge(ada_added, 1)
            first_units(0, (("A", 0, ps[:, 1:3, :]), ("B", 0, AB67)), context=ps[:, 0, 0:NC_])
            head(0)
            with pe.Fori(1, NH - 1) as hd:
                head(hd)
            head(NH - 1, last=True)

            pe.wait_ge(gate_evac, 4 * NH)
            for ks in (range(KT - 1), range(KT - 1, KT)):
                for s, banks in (("A", AB01), ("B", AB23)):
                    pe.wait_ge(w_ready[s], NH + 1)
                    for k in ks:
                        wait_h(pe, 1, 0, k)
                        mm = product(s, k * P, [piece(banks, H_hi, H_lo, k, h) for h in range(2)],
                                     k == 0, k == KT - 1)
                    if KT - 1 in ks:
                        mm.then_inc(unit_done[s], 1)
            ada_columns(4 * NH, 4, ps[:, 4, 0:4])
            with pe.Fori(1, 4) as i:
                pe.wait_ge(y_evac, 2 * i - 1)
                unit("A", NH + i, AB01)
                pe.wait_ge(y_evac, 2 * i)
                unit("B", NH + i, AB23)
            pe.wait_ge(ada_added, NH + 1)
            norms(1, 2)

            def down(L, j):
                c = FJ * L + j
                pe.wait_ge(w_ready["C"], c + 1)
                pe.wait_ge(f_ready, c + 1)
                for m in range(KT):
                    if m < 2:
                        if not (isinstance(c, int) and c == 0):
                            pe.wait_ge(d_added, 8 * c + 8 * L)
                        if m == 0 and L == 0:
                            pe.wait_ge(ada_added, NH + 2 + j)
                    elif m == 2:
                        pe.wait_ge(u_evac, c + 2)
                    else:
                        pe.wait_ge(d_added, 8 * c + 8 * L + m - 2)
                    b = (4, 6, 0)[m % 3]
                    product("C", m * P, [(ps[:, b + h], F_hi[:, hs(h)], F_lo[:, hs(h)]) for h in range(2)])\
                        .then_inc(d_done, 1)

            def down_last(L):
                c = FJ * (L + 1) - 1
                pe.wait_ge(w_ready["C"], c + 1)
                pe.wait_ge(f_ready, c + 1)
                pe.wait_ge(d_added, 8 * c + 8 * L)
                if L == 0:
                    pe.wait_ge(ada_added, NH + 1 + FJ)
                for h in range(2):
                    for m in range(KT):
                        n = 8 * h + m
                        if n >= 4:
                            pe.wait_ge(d_added, 8 * c + 8 * L + n - 3)
                        product("C", m * P, [(ps[:, 4 + n % 4], F_hi[:, hs(h)], F_lo[:, hs(h)])])\
                            .then_inc(d_done, 1)

            def ffn_step(L, j):
                n, c = N_FFN[L] + j, FJ * L + j
                if not (isinstance(j, int) and j == 0):
                    pe.wait_ge(u_evac, c)
                    if not (isinstance(j, int) and j == 1):
                        pe.wait_ge(d_added, 8 * c + 8 * L - 10)
                    unit("A", n, AB01)
                    down(L, j - 1)
                    pe.wait_ge(f_mul, c)
                    unit("B", n, AB23)
                if L == 0:
                    if not (isinstance(j, int) and j == 0):
                        pe.wait_ge(d_added, 8 * j - 1)
                    ada_columns(4 * NH + 2 * j + 2, 2, ps[:, 4, 0:2])

            def ffn(L):
                first_units(2 + 2 * L, (("A", N_FFN[L], AB01), ("B", N_FFN[L], AB23)))
                ffn_step(L, 0)
                ffn_step(L, 1)
                with pe.Fori(2, FJ) as j:
                    ffn_step(L, j)
                down_last(L)
                norms(3 + 4 * L)

            ffn(0)
            norms(4)

            for p, mt in enumerate(POOL_OUT):
                g, m = divmod(mt, 2)
                s, e = ("A", "p") if g < 2 else ("B", "v")
                pe.wait_ge(w_ready[s], N_POOL + 1)
                if p >= 2:
                    pe.wait_ge(y_evac, 8 + p - 1)
                banks = (AB01, AB23)[p % 2]
                pe.wait_ge(diff_ready[e], 2 * (g % 2) + 2)
                for k in range(2):
                    mm = product(s, (g % 2) * 512 + k * 256 + m * P,
                                 [piece(banks, H_hi, H_lo, 2 * g + k, h) for h in range(2)], k == 0, k == 1)
                mm.then_inc(unit_done[s] if mt in (3, 7) else pool_mm, 1)
            norms(5, 6)
            ffn(1)

        @block.scalar
        def _(act):
            A = act.activation

            def round_hi(s, n):
                act.wait_ge(raw_full[s], 16 * n + 16)
                if not (isinstance(n, int) and n == 0):
                    act.wait_ge(unit_done[s], n)
                A(W_hi[s][:], raw[s][:], ACT.Copy).then_inc(w_hi[s], 1)

            def round_down(L, j):
                c = FJ * L + j
                act.wait_ge(raw_full["C"], 16 * c + 16)
                if not (isinstance(c, int) and c == 0):
                    act.wait_ge(d_done, 8 * c + 8 * L)
                A(W_hi["C"][:], raw["C"][:], ACT.Copy).then_inc(w_hi["C"], 1)

            def square(q, h, p, src):
                n = 2 * q + h
                if p < 2:
                    dst = acc[p]
                    if q:
                        act.wait_ge(ssq_done, n - 1)
                else:
                    dst = S[p % 2]
                    if p >= 4:
                        act.wait_ge((sum_even, sum_odd)[p % 2], 3 * n + p // 2 - 1)
                A(dst[:, hs(h)], src[:, hs(h)], ACT.Square).then_inc(sq_made, 1)

            def norm_root(q, h):
                act.wait_ge(ssq_done, 2 * q + h + 1)
                A(rms[:, 4 * h:4 * h + 4], ps[:, ssq_bank(q, h), 0:4], ACT.Sqrt, scale=1.0 / D,
                  bias=eps[:, 0:1]).then_inc(rms_made, 1)

            def fill_h(i, L, ffn_part, h):
                for k in range(KT):
                    act.wait_ge(x_scaled, 16 * i + 8 * h + k + 1)
                    c = 48 * L + 24 * ffn_part + k
                    if k % 2 == 0:
                        A(H_hi[:, k, hs(h)], Y[:, k, hs(h)], ACT.Identity, bias=M[:, c:c + 1]).then_inc(h_hi, 1)
                    else:
                        A(Y[:, k, hs(h)], Y[:, k, hs(h)], ACT.Identity, bias=M[:, c:c + 1]).then_inc(affine_made, 1)
                        act.wait_ge(affine_made, AFFINE_BASE[i] + 4 * h + k // 2 + 1)
                        A(H_hi[:, k, hs(h)], Y[:, k, hs(h)], ACT.Copy).then_inc(h_hi, 1)

            act.wait_ge(par_full, 16)
            A(silu_c[:], col("cond", 0, 16).rearrange("p (k v) -> p k v", v=2), ACT.Silu).then_inc(silu_done, 1)
            A(sp[:, 0], col("lam", 0, 16), ACT.Abs).then_inc(softplus_step, 1)
            act.wait_ge(softplus_step, 1)
            A(sp[:, 1], sp[:, 0], ACT.Exp, scale=-1.0).then_inc(softplus_step, 1)
            act.wait_ge(softplus_step, 3)
            A(sp[:, 3], sp[:, 2], ACT.Ln).then_inc(softplus_step, 1)
            for h in range(2):
                for m in range(KT):
                    act.wait_ge(x_full[m // 2], 16)
                    square(0, h, m, Y[:, m])
            act.wait_ge(ctx_full, 16)
            A(ctx_sq[:], ctx_x[:], ACT.Square).then_inc(csq_made, 1)
            act.wait_ge(memset_done, 3)
            norm_root(0, 0)
            norm_root(0, 1)
            round_hi("A", 0)
            round_hi("B", 0)
            act.wait_ge(cssq_done, 1)
            A(rms_c[:], ps[:, 0, 0:2], ACT.Sqrt, scale=1.0 / D, bias=eps[:, 0:1]).then_inc(crms_made, 1)
            act.wait_ge(coef_ready, 1)
            act.wait_ge(cscaled, 1)
            for k in range(KT):
                A(ctx_x[:, k], ctx_x[:, k], ACT.Identity, scale=cAc[:, k:k + 1], bias=Mc[:, k:k + 1])\
                    .then_inc(caffine, 1)
            act.wait_ge(caffine, KT)
            A(Hc_hi[:], ctx_x[:], ACT.Copy).then_inc(chi, 1)
            for h in range(2):
                fill_h(0, 0, 0, h)

            def head(hd):
                first = isinstance(hd, int) and hd == 0
                act.wait_ge(unit_done["A"], hd + 1)
                if not first:
                    act.wait_ge(u_made, hd)
                A(rec[:, 2:2 + NC_], ps[:, 0, 0:NC_], ACT.Copy)
                A(rec[:, 2 + LAT:2 + TA], flat(ps[:, 1:3, :]), ACT.Copy).then_inc(rec_evac, 1)
                round_hi("A", hd + 1)
                act.wait_ge(unit_done["B"], hd + 1)
                A(Y[:, hd], flat(AB67), ACT.Gelu_apprx_tanh).then_inc(g_made, 1)
                round_hi("B", hd + 1)
                for gi in range(4):
                    d, b = gi // 2, 3 if gi % 2 == 0 else 0
                    dst, name = ((RA[d], "gate_a_b"), (IB[d], "gate_x_b"))[gi % 2]
                    act.wait_ge(gate_done, 4 * hd + gi + 1)
                    if not first:
                        act.wait_ge(scan_done, 2 * hd - 1 + d)
                    A(dst[:, 0:NC_], ps[:, b, 0:NC_], ACT.Sigmoid, bias=col(name, d * NH + hd))
                    A(dst[:, LAT:TA], flat(ps[:, b + 1:b + 3, :]), ACT.Sigmoid, bias=col(name, d * NH + hd))\
                        .then_inc(gate_evac, 1)
                for d in range(2):
                    act.wait_ge(gate_evac, 4 * hd + 2 * d + 2)
                    if not first:
                        act.wait_ge(gy_made, hd)
                    A(TH[d][:], RA[d][:], ACT.Tanh, scale=s_tanh[:, bass.ds(d * NH + hd, 1)])\
                        .then_inc(tanh_made, 1)
                for d in range(2):
                    A(RA[d][:], RA[d][:], ACT.Exp, scale=s_exp[:, bass.ds(d * NH + hd, 1)]).then_inc(exp_made, 1)
                for d in range(2):
                    act.wait_ge(tanh_made, 2 * hd + d + 1)
                    A(TH[d][:], TH[d][:], ACT.Sqrt).then_inc(sqrt_made, 1)

            act.wait_ge(lam_ready, 1)
            act.wait_ge(zeros_ready, 1)
            head(0)
            with act.Fori(1, NH) as hd:
                head(hd)
            for k in range(KT):
                act.wait_ge(gy_made, k + 1)
                A(H_hi[:, k], Y[:, k], ACT.Copy).then_inc(h_hi, 1)
            for m in range(KT):
                s, n = "AB"[m % 2], NH + m // 2
                act.wait_ge(unit_done[s], n + 1)
                A(Y[:, m], flat((AB01, AB23)[m % 2]), ACT.Copy).then_inc(y_evac, 1)
                round_hi(s, n + 1)
                act.wait_ge(y_evac, m + 1)
                square(1, 0, m, Y[:, m])
            round_down(0, 0)

            def squares_y(q, h):
                for p, m in enumerate(tiles_of(q)):
                    square(q, h, p, Y[:, m])

            def squares_x(q, i, h, ms):
                for m in ms:
                    wait_new(act, i, h, m)
                    square(q, h, m, X[:, m])

            def next_stream(q, i, out_squares, fill):
                norm_root(q, 0)
                if out_squares:
                    squares_y(q, 1)
                squares_x(q + 1, i, 0, range(4))
                norm_root(q, 1)
                squares_x(q + 1, i, 0, range(4, KT))
                norm_root(q + 1, 0)
                squares_x(q + 1, i, 1, range(4))
                if fill is not None:
                    fill(0)
                squares_x(q + 1, i, 1, range(4, KT))
                norm_root(q + 1, 1)
                if fill is not None:
                    fill(1)

            def fill_ffn(L, h):
                act.wait_ge(coef_ready, 2 + L)
                fill_h(1 + 2 * L, L, 1, h)

            def ffn_step(L, j):
                n, c = N_FFN[L] + j, FJ * L + j
                static = isinstance(j, int)
                last = static and n + 1 == N_AB
                act.wait_ge(unit_done["A"], n + 1)
                if not (static and c == 0):
                    act.wait_ge(conv_done, c)
                A(Ub[:, 1:T + 1], flat(AB01), ACT.Copy).then_inc(u_evac, 1)
                act.wait_ge(u_evac, c + 1)
                if not (static and c == 0):
                    act.wait_ge(f_mul, c)
                A(S[0][:], Ub[:, 1:T + 1], ACT.Identity, scale=col("ffn_conv_w", 72 * L + 24 + j),
                  bias=col("ffn_conv_b", 24 * L + j)).then_inc(tap_done, 1)
                if not last:
                    round_hi("A", n + 1)
                act.wait_ge(conv_done, c + 1)
                A(S[0][:], S[0][:], ACT.Gelu_apprx_tanh).then_inc(gelu_done, 1)
                if not (static and c == 0):
                    round_down(L, j)
                act.wait_ge(f_mul, c + 1)
                A(F_hi[:], S[1][:], ACT.Copy).then_inc(f_hi, 1)
                if not last:
                    round_hi("B", n + 1)

            def ffn(L):
                ffn_step(L, 0)
                with act.Fori(1, FJ - 1) as j:
                    ffn_step(L, j)
                ffn_step(L, FJ - 1)
                for h in range(2):
                    for m in range(KT):
                        act.wait_ge(d_added, 8 * (FJ * (L + 1) - 1) + 8 * L + 8 * h + m + 1)
                        square(3 + 4 * L, h, m, Y[:, m])

            next_stream(1, 0, True, lambda h: fill_ffn(0, h))
            ffn(0)
            next_stream(3, 1, False, None)

            def load_col(e, t):
                k, pad = POOL_TILES[e][t], {"p": 2, "v": 8}[e]
                dst = {"p": col_p, "v": col_v}[e][:, :, pad:pad + GW]
                if t == 0:
                    A(dst, Y[:, k].rearrange("p (r c) -> p r c", c=GW), ACT.Identity, bias=M[:, 48 + k:49 + k])\
                        .then_inc(col_loaded[e], 1)
                else:
                    act.wait_ge(tile_affine, k + 1)
                    act.wait_ge(pool_step[e], pool_steps(e, t - 1) + 1)
                    A(dst, Y[:, k].rearrange("p (r c) -> p r c", c=GW), ACT.Copy).then_inc(col_loaded[e], 1)

            act.wait_ge(coef_ready, 3)
            act.wait_ge(pads_ready, 1)
            for e in "pv":
                act.wait_ge(x_scaled, 32 + 8 + POOL_TILES[e][0] + 1)
                load_col(e, 0)
            for k in range(KT):
                act.wait_ge(x_scaled, 32 + 8 + k + 1)
                A(Y[:, k], Y[:, k], ACT.Identity, bias=M[:, 48 + k:49 + k]).then_inc(tile_affine, 1)
            for e in "pv":
                load_col(e, 1)
            for t in range(4):
                for e in "pv":
                    act.wait_ge(diff_made[e], t + 1)
                    k = POOL_TILES[e][t]
                    A(H_hi[:, k], Y[:, k], ACT.Copy).then_inc(diff_hi[e], 1)
                    if t + 2 < 4:
                        load_col(e, t + 2)
            for p, mt in enumerate(POOL_OUT):
                if mt in (3, 7):
                    act.wait_ge(unit_done["AB"[mt // 4]], N_POOL + 1)
                else:
                    act.wait_ge(pool_mm, sum(m not in (3, 7) for m in POOL_OUT[:p + 1]))
                A(Y[:, mt], flat((AB01, AB23)[p % 2]), ACT.Identity, scale=col("pool_scale", mt),
                  bias=pbs[:, mt:mt + 1]).then_inc(y_evac, 1)
                act.wait_ge(y_evac, 8 + p + 1)
                square(5, 0, p, Y[:, mt])
                if mt == 7:
                    round_hi("B", N_FFN[1])
            round_hi("A", N_FFN[1])
            next_stream(5, 2, True, lambda h: fill_ffn(1, h))
            ffn(1)
            norm_root(7, 0)
            norm_root(7, 1)

        def pool_tile(eng, e, t):
            k = POOL_TILES[e][t]
            w = WINDOWS[k // 2]
            pad, off, colg, row, pts, cnt = {
                "p": (2, 0, col_p, row_p, (pt_p, pt_p), S[0]), "v": (8, 1, col_v, row_v, (pt0, pt1), S[1])}[e]
            n = pool_steps(e, t)
            inner = row[:, pad:pad + GR, :]
            TT = eng.tensor_tensor
            eng.wait_ge(col_loaded[e], t + 1)
            if t:
                eng.wait_ge(diff_made[e], t)
            src = colg
            for stage in range(window_stages(w)):
                s = 2 << stage
                lo, hi = pad - (w - s) // 2, pad + GW + (w - s) // 2
                left, right = (1, 0) if s == 2 else (s // 4, -(s // 4))
                if s == w:
                    nxt, dst = None, inner
                else:
                    nxt = pts[stage % 2][:, 0:GR * (GW + 2 * pad)].rearrange("p (r c) -> p r c", c=GW + 2 * pad)
                    dst = nxt[:, :, lo:hi]
                if n:
                    eng.wait_ge(pool_step[e], n)
                TT(dst, src[:, :, lo - left:hi - left], src[:, :, lo - right:hi - right], ALU.add)\
                    .then_inc(pool_step[e], 1)
                n += 1
                src = nxt
            src, at = row[:].rearrange("p r c -> p (r c)"), 0
            for stage in range(window_stages(w)):
                s = 2 << stage
                lo, hi = pad - (w - s) // 2, pad + GR + (w - s) // 2
                left, right = (1, 0) if s == 2 else (s // 4, -(s // 4))
                if s == w and s > 2:
                    nxt, nxt_at = row[:].rearrange("p r c -> p (r c)"), 0
                else:
                    nxt, nxt_at = pts[stage % 2][:], off
                eng.wait_ge(pool_step[e], n)
                TT(nxt[:, (lo - nxt_at) * GW:(hi - nxt_at) * GW],
                   src[:, (lo - left - at) * GW:(hi - left - at) * GW],
                   src[:, (lo - right - at) * GW:(hi - right - at) * GW], ALU.add).then_inc(pool_step[e], 1)
                n += 1
                src, at = nxt, nxt_at
            own = src[:, (pad - at) * GW:(pad + GR - at) * GW]
            eng.wait_ge(pool_step[e], n)
            eng.wait_ge(cnt_full[e], 16 * (t // 2 + 1))
            TT(own, own, cnt[:], ALU.mult).then_inc(pool_step[e], 1)
            eng.wait_ge(pool_step[e], n + 1)
            eng.wait_ge(tile_affine, k + 1)
            TT(Y[:, k], own, Y[:, k], ALU.subtract).then_inc(diff_made[e], 1)

        def lo_of_diff(eng, e, t):
            k = POOL_TILES[e][t]
            eng.wait_ge(diff_hi[e], t + 1)
            eng.tensor_tensor(H_lo[:, k], Y[:, k], H_hi[:, k].bitcast(F32), ALU.subtract)\
               .then_inc(diff_ready[e], 1)

        @block.gpsimd
        def _(pool):
            TT = pool.tensor_tensor

            def lo_of_unit(s, n):
                pool.wait_ge(w_hi[s], n + 1)
                TT(W_lo[s][:], raw[s][:], W_hi[s][:].bitcast(F32), ALU.subtract).then_inc(w_ready[s], 1)

            def lo_of_odd(i, h):
                for k in range(1, KT, 2):
                    pool.wait_ge(h_hi, H_BASE[FILL[i]] + 8 * h + k + 1)
                    TT(H_lo[:, k, hs(h)], Y[:, k, hs(h)], H_hi[:, k, hs(h)].bitcast(F32), ALU.subtract)\
                        .then_inc(h_ready[1], 1)

            def odd_sum(q, h, p):
                n = 2 * q + h
                pool.wait_ge(sq_made, 8 * n + p + 1)
                if p > 3:
                    pool.wait_ge(sum_odd, 3 * n + p // 2 - 1)
                TT(acc[1][:, hs(h)], acc[1][:, hs(h)], S[1][:, hs(h)], ALU.add).then_inc(sum_odd, 1)

            def odd_sums(q, h):
                for p in range(3, KT, 2):
                    odd_sum(q, h, p)

            def ada_products(p):
                for i in range(2):
                    pool.wait_ge(e_full[i], 16 * p + 16)
                    TT(E[i][:], E[i][:], silu_c[:, :, 0:1].to_broadcast([P, KT, P]), ALU.mult)\
                        .then_inc(e_mul, 1)

            def add_odd(i, h, ms):
                for m in ms:
                    if i == 0 and h == 0:
                        pool.wait_ge(res_full[m // 2], 16)
                    pool.wait_ge(y_scaled, 16 * i + 8 * h + m + 1)
                    TT(X[:, m, hs(h)], X[:, m, hs(h)], Y[:, m, hs(h)], ALU.add).then_inc(x_new[1], 1)

            def next_stream(q, i, sums_ready, lo, pads=None):
                if sums_ready:
                    odd_sums(q, 1)
                add_odd(i, 0, (1, 3))
                if not sums_ready:
                    odd_sums(q, 1)
                add_odd(i, 0, (5, 7))
                add_odd(i, 1, (1, 3))
                odd_sums(q + 1, 0)
                if lo:
                    lo(0)
                add_odd(i, 1, (5, 7))
                odd_sums(q + 1, 1)
                if lo:
                    lo(1)

            def fill_ffn(L, h):
                if h == 0:
                    pool.memset(Ub[:, 0:1], 0.0)
                    pool.memset(Ub[:, T + 1:T + 2], 0.0)
                lo_of_odd(1 + 2 * L, h)

            pool.memset(ones[:], 1.0).then_inc(memset_done, 1)
            pool.memset(eps[:], EPS).then_inc(memset_done, 1)
            pool.memset(s_exp[:], 0.0).then_inc(memset_done, 1)
            odd_sums(0, 0)
            odd_sums(0, 1)
            lo_of_unit("A", 0)
            lo_of_unit("B", 0)
            pool.wait_ge(chi, 1)
            TT(Hc_lo[:], ctx_x[:], Hc_hi[:].bitcast(F32), ALU.subtract).then_inc(hc_ready, 1)
            lo_of_odd(0, 0)
            pool.wait_ge(hc_ready, 1)
            pool.wait_ge(rb_done, 2)
            for t in (rec[:, 0:2], rec[:, 2 + NC_:2 + LAT], rec[:, 2 + TA:3 + TA],
                      *(b[:, NC_:LAT] for b in (*RA, *IB))):
                ms = pool.memset(t, 0.0)
            ms.then_inc(zeros_ready, 1)
            lo_of_odd(0, 1)

            def head(hd):
                ada_products(2 * hd)
                lo_of_unit("A", hd + 1)
                lo_of_unit("B", hd + 1)
                pool.wait_ge(u_made, hd + 1)
                for d in range(2):
                    pool.wait_ge(gate_evac, 4 * hd + 2 * d + 2)
                    TT(IB[d][:], IB[d][:], u[:], ALU.mult).then_inc(iu_made, 1)
                ada_products(2 * hd + 1)

            head(0)
            with pool.Fori(1, NH) as hd:
                head(hd)
            for k in range(KT):
                pool.wait_ge(h_hi, H_BASE[1] + k + 1)
                TT(H_lo[:, k], Y[:, k], H_hi[:, k].bitcast(F32), ALU.subtract).then_inc(h_ready[k % 2], 1)
            for m in range(KT):
                lo_of_unit("AB"[m % 2], NH + m // 2 + 1)
                if m in (3, 5, 7):
                    odd_sum(1, 0, m)
            lo_of_unit("C", 0)

            def ffn_step(L, j):
                n, c = N_FFN[L] + j, FJ * L + j
                static = isinstance(j, int)
                last = static and n + 1 == N_AB
                if not last:
                    lo_of_unit("A", n + 1)
                if L == 0:
                    ada_products(2 * NH + j)
                if not (static and c == 0):
                    lo_of_unit("C", c)
                pool.wait_ge(f_hi, c + 1)
                TT(F_lo[:], S[1][:], F_hi[:].bitcast(F32), ALU.subtract).then_inc(f_ready, 1)
                if not last:
                    lo_of_unit("B", n + 1)

            def ffn(L):
                ffn_step(L, 0)
                with pool.Fori(1, FJ - 1) as j:
                    ffn_step(L, j)
                ffn_step(L, FJ - 1)
                odd_sums(3 + 4 * L, 0)

            next_stream(1, 0, False, lambda h: fill_ffn(0, h))
            ffn(0)
            next_stream(3, 1, True, None)
            pool.wait_ge(rb_done, 10)
            for grid in (col_p, row_p, col_v):
                pool.memset(grid[:], 0.0)
            pool.memset(row_v[:], 0.0).then_inc(pads_ready, 1)
            for t in range(4):
                pool_tile(pool, "p", t)
                if t:
                    lo_of_diff(pool, "p", t - 1)
            lo_of_diff(pool, "p", 3)
            odd_sums(5, 0)
            lo_of_unit("B", N_FFN[1])
            lo_of_unit("A", N_FFN[1])
            next_stream(5, 2, False, lambda h: fill_ffn(1, h))
            ffn(1)
            odd_sums(7, 1)
            add_odd(3, 0, (1, 3, 5, 7))
            add_odd(3, 1, (1, 3, 5, 7))

        @block.vector
        def _(dve):
            TT, STT, TS = dve.tensor_tensor, dve.scalar_tensor_tensor, dve.tensor_scalar

            def even_sum(q, h, p):
                n = 2 * q + h
                dve.wait_ge(sq_made, 8 * n + p + 1)
                if p > 2:
                    dve.wait_ge(sum_even, 3 * n + p // 2 - 1)
                TT(acc[0][:, hs(h)], acc[0][:, hs(h)], S[0][:, hs(h)], ALU.add).then_inc(sum_even, 1)

            def even_sums(q, h):
                for p in range(2, KT, 2):
                    even_sum(q, h, p)

            def norm_diagonal(q, h):
                n, c = 2 * q + h, slice(4 * h, 4 * h + 4)
                dve.wait_ge(rms_made, n + 1)
                dve.reciprocal(rstd[:, c], rms[:, c]).then_inc(rstd_made, 1)
                dve.wait_ge(rstd_made, n + 1)
                if q:
                    dve.wait_ge(rb_done, n - 1)
                TT(diag[:, c], ident[:].unsqueeze(1).to_broadcast([P, 4, P]),
                   rstd[:, c].unsqueeze(2).to_broadcast([P, 4, P]), ALU.mult).then_inc(diag_made, 1)

            def ada_sums(p, at, n_used):
                dve.wait_ge(ada_out, n_used)
                for i in range(2):
                    dve.wait_ge(e_mul, 2 * p + i + 1)
                    dve.tensor_reduce(red[:, at + i], E[i][:].rearrange("p k m -> p m k"),
                                      mybir.AxisListType.X, ALU.add).then_inc(red_made, 1)

            def add_ada_bias(out, first, n, count):
                dve.wait_ge(ada_out, count)
                TT(M[:, bass.ds(first, n)], out, col("ada_b", first, n), ALU.add).then_inc(ada_added, 1)

            def coefs(i, L, ffn_part):
                a, o = 48 * L + 24 * ffn_part, 8 * L
                STT(cA[:, i], M[:, a + 8:a + 16], 1.0,
                    col(("npre_mix", "npre_ffn")[ffn_part], o, 8), ALU.add, ALU.mult)

            def gates(i, L, ffn_part):
                a, o = 48 * L + 24 * ffn_part, 8 * L
                return TT(cG[:, i], M[:, a + 16:a + 24], col(("npost_mix", "npost_ffn")[ffn_part], o, 8), ALU.mult)

            def scale_tiles(i, q, h, src, fill=True):
                dve.wait_ge(rb_done, 2 * q + h + 1)
                for k in range(KT + (4 if fill else 0)):
                    if k < KT:
                        STT(Y[:, k, hs(h)], src[:, k, hs(h)], cA[:, i, k:k + 1], ps[:, rb_bank(q, h)],
                            ALU.mult, ALU.mult).then_inc(x_scaled, 1)
                    if fill and k >= 4 and k % 2 == 0:
                        e = k - 4
                        c = {0: 0, 1: 24, 3: 72}[i] + e
                        dve.wait_ge(h_hi, H_BASE[FILL[i]] + 8 * h + e + 1)
                        STT(H_lo[:, e, hs(h)], Y[:, e, hs(h)], M[:, c:c + 1], H_hi[:, e, hs(h)].bitcast(F32),
                            ALU.add, ALU.subtract).then_inc(h_ready[0], 1)

            def gate_tiles(i, q, h, ms):
                dve.wait_ge(rb_done, 2 * q + h + 1)
                for m in ms:
                    STT(Y[:, m, hs(h)], Y[:, m, hs(h)], cG[:, i, m:m + 1], ps[:, rb_bank(q, h)],
                        ALU.mult, ALU.mult).then_inc(y_scaled, 1)
                    if m % 2:
                        if i == 0 and h == 0:
                            dve.wait_ge(res_full[m // 2], 16)
                        dve.wait_ge(y_scaled, 16 * i + 8 * h + m)
                        TT(X[:, m - 1, hs(h)], X[:, m - 1, hs(h)], Y[:, m - 1, hs(h)], ALU.add)\
                            .then_inc(x_new[0], 1)

            def next_stream(q, i, sums_ready, fill):
                norm_diagonal(q, 0)
                gate_tiles(i, q, 0, range(KT))
                if not sums_ready:
                    even_sums(q, 1)
                norm_diagonal(q, 1)
                gate_tiles(i, q, 1, range(4))
                even_sums(q + 1, 0)
                norm_diagonal(q + 1, 0)
                scale_tiles(i + 1, q + 1, 0, X, fill)
                gate_tiles(i, q, 1, range(4, KT))
                even_sums(q + 1, 1)
                norm_diagonal(q + 1, 1)
                scale_tiles(i + 1, q + 1, 1, X, fill)

            dve.wait_ge(softplus_step, 2)
            TS(sp[:, 2], sp[:, 1], 1.0, None, ALU.add).then_inc(softplus_step, 1)
            dve.wait_ge(softplus_step, 4)
            TS(sp[:, 4], sp[:, 2], -1.0, None, ALU.add).then_inc(softplus_step, 1)
            dve.wait_ge(softplus_step, 5)
            TS(sp[:, 5], sp[:, 4], 0.0, None, ALU.is_equal).then_inc(softplus_step, 1)
            dve.wait_ge(softplus_step, 6)
            TT(sp[:, 3], sp[:, 3], sp[:, 5], ALU.add).then_inc(softplus_step, 1)
            TT(sp[:, 4], sp[:, 4], sp[:, 5], ALU.add).then_inc(softplus_step, 1)
            dve.wait_ge(softplus_step, 8)
            dve.reciprocal(sp[:, 6], sp[:, 4]).then_inc(softplus_step, 1)
            TT(sp[:, 3], sp[:, 3], sp[:, 1], ALU.mult).then_inc(softplus_step, 1)
            dve.wait_ge(softplus_step, 10)
            TT(sp[:, 3], sp[:, 3], sp[:, 6], ALU.mult).then_inc(softplus_step, 1)
            TS(sp[:, 7], col("lam", 0, 16), -1.0, 0.0, ALU.mult, ALU.max).then_inc(softplus_step, 1)
            dve.wait_ge(softplus_step, 12)
            TT(sp[:, 3], sp[:, 3], sp[:, 7], ALU.add).then_inc(softplus_step, 1)
            dve.wait_ge(softplus_step, 13)
            dve.wait_ge(memset_done, 3)
            TS(s_tanh[:], sp[:, 3], 0.5 * RG_C, None, ALU.mult)
            TS(s_exp[:], sp[:, 3], -RG_C, None, ALU.mult).then_inc(lam_ready, 1)
            TT(pbs[:], col("pool_b", 0, 8), col("pool_scale", 0, 8), ALU.mult)
            even_sums(0, 0)
            even_sums(0, 1)
            dve.wait_ge(const_full, 16)
            norm_diagonal(0, 0)
            norm_diagonal(0, 1)
            dve.wait_ge(crms_made, 1)
            dve.reciprocal(rstd_c[:], rms_c[:]).then_inc(crstd_made, 1)
            dve.wait_ge(crstd_made, 1)
            TT(diag_c[:], ident[:].unsqueeze(1).to_broadcast([P, 2, P]),
               rstd_c[:].unsqueeze(2).to_broadcast([P, 2, P]), ALU.mult).then_inc(cdiag_made, 1)
            dve.wait_ge(crb_done, 1)
            TT(ctx_x[:], ctx_x[:], ps[:, 3, 0:NC_].unsqueeze(1).to_broadcast([P, KT, NC_]), ALU.mult)\
                .then_inc(cscaled, 1)
            dve.wait_ge(ada_out, 1)
            first = ps[:, 2, 0:2 * ADA0].rearrange("p (m v) -> p m v", v=2)
            TT(M[:, 0:ADA0], first[:, :, 0], col("ada_b", 0, ADA0), ALU.add)
            TT(Mc[:], first[:, :, 1], col("ada_b", 0, ADA0), ALU.add).then_inc(ada_added, 1)
            dve.wait_ge(ada_added, 1)
            coefs(0, 0, 0)
            STT(cAc[:], Mc[:, 8:16], 1.0, col("npre_mix", 0, 8), ALU.add, ALU.mult).then_inc(coef_ready, 1)
            dve.wait_ge(coef_ready, 1)
            scale_tiles(0, 0, 0, Y)
            scale_tiles(0, 0, 1, Y)

            def convolve(hd):
                dve.wait_ge(rec_evac, hd + 1)
                if not (isinstance(hd, int) and hd == 0):
                    dve.wait_ge(gate_done, 4 * hd)
                    dve.wait_ge(iu_made, 2 * hd)
                TS(u[:], rec[:, 0:TA], col("rg_conv_w", hd), col("rg_conv_b", hd), ALU.mult, ALU.add)\
                    .then_inc(conv_step, 1)
                for tap in range(1, 4):
                    dve.wait_ge(conv_step, 3 * hd + tap)
                    STT(u[:], rec[:, tap:tap + TA], col("rg_conv_w", tap * NH + hd), u[:], ALU.mult, ALU.add)\
                        .then_inc(conv_step if tap < 3 else u_made, 1)

            def scans(hd, d):
                n = 2 * hd + d + 1
                dve.wait_ge(sqrt_made, n)
                STT(TH[d][:], RA[d][:], 1.0, TH[d][:], ALU.add, ALU.mult).then_inc(mult_made, 1)
                dve.wait_ge(mult_made, n)
                dve.wait_ge(iu_made, n)
                TT(IB[d][:], IB[d][:], TH[d][:], ALU.mult).then_inc(b_made, 1)
                dve.wait_ge(b_made, n)
                rev = slice(None, None, -1 if d else 1)
                a, b, h = ([t[:, 0:NC_][:, rev], t[:, LAT:TA][:, rev]] for t in (RA[d], IB[d], TH[d]))
                dve.tensor_tensor_scan(h[0], a[0], b[0], 0.0, ALU.mult, ALU.add).then_inc(scan_ctx, 1)
                dve.wait_ge(scan_ctx, n)
                dve.tensor_tensor_scan(h[1], a[1], b[1], h[0][:, NC_ - 1:NC_], ALU.mult, ALU.add)\
                    .then_inc(scan_done, 1)

            def combine(hd):
                dve.wait_ge(scan_done, 2 * hd + 2)
                TT(TH[0][:, LAT:TA], TH[0][:, LAT:TA], TH[1][:, LAT:TA], ALU.add).then_inc(ysum_made, 1)
                dve.wait_ge(ysum_made, hd + 1)
                dve.wait_ge(g_made, hd + 1)
                TT(Y[:, hd], Y[:, hd], TH[0][:, LAT:TA], ALU.mult).then_inc(gy_made, 1)

            def head(hd, last=False):
                ada_sums(2 * hd, 0, hd + 1)
                ada_sums(2 * hd + 1, 2, hd + 1)
                scans(hd, 0)
                if not last:
                    convolve(hd + 1)
                    add_ada_bias(ps[:, 3, 0:4], ADA0 + 4 * hd, 4, hd + 2)
                scans(hd, 1)
                combine(hd)

            dve.wait_ge(zeros_ready, 1)
            convolve(0)
            head(0)
            with dve.Fori(1, NH - 1) as hd:
                head(hd)
            head(NH - 1, last=True)
            add_ada_bias(ps[:, 4, 0:4], ADA0 + 4 * (NH - 1), 4, NH + 1)
            dve.wait_ge(ada_added, NH + 1)
            coefs(1, 0, 1)
            gates(0, 0, 0)
            gates(1, 0, 1).then_inc(coef_ready, 1)
            even_sums(1, 0)
            dve.wait_ge(coef_ready, 2)
            next_stream(1, 0, False, True)

            def add_down(L, j):
                for m in range(KT):
                    dve.wait_ge(d_done, 8 * (FJ * L + j) + 8 * L + m + 1)
                    b = (4, 6, 0)[m % 3]
                    if isinstance(j, int) and j == 0:
                        dve.tensor_copy(Y[:, m], flat(ps[:, b:b + 2, :])).then_inc(d_added, 1)
                    else:
                        TT(Y[:, m], Y[:, m], flat(ps[:, b:b + 2, :]), ALU.add).then_inc(d_added, 1)

            def add_down_last(L):
                q = 3 + 4 * L
                for n in range(2 * KT):
                    h, m = divmod(n, KT)
                    dve.wait_ge(d_done, 8 * (FJ * (L + 1) - 1) + 8 * L + n + 1)
                    TT(Y[:, m, hs(h)], Y[:, m, hs(h)], ps[:, 4 + n % 4], ALU.add).then_inc(d_added, 1)
                    if n in (4, 6, 8):
                        even_sum(q, 0, n - 2)
                    if n in (12, 14):
                        even_sum(q, 1, n - 10)
                even_sum(q, 1, 6)

            def ffn_step(L, j):
                n, c = N_FFN[L] + j, FJ * L + j
                at0 = isinstance(j, int) and j == 0
                if not at0:
                    add_down(L, j - 1)
                dve.wait_ge(tap_done, c + 1)
                STT(S[0][:], Ub[:, 0:T], col("ffn_conv_w", 72 * L + j), S[0][:], ALU.mult, ALU.add)\
                    .then_inc(conv_a, 1)
                dve.wait_ge(conv_a, c + 1)
                STT(S[0][:], Ub[:, 2:T + 2], col("ffn_conv_w", 72 * L + 48 + j), S[0][:], ALU.mult, ALU.add)\
                    .then_inc(conv_done, 1)
                if L == 0:
                    ada_sums(2 * NH + j, 0, NH + 1 + j)
                dve.wait_ge(gelu_done, c + 1)
                dve.wait_ge(unit_done["B"], n + 1)
                if not (isinstance(c, int) and c == 0):
                    dve.wait_ge(f_ready, c)
                TT(S[1][:], S[0][:], flat(AB23), ALU.mult).then_inc(f_mul, 1)
                if L == 0:
                    add_ada_bias(ps[:, 4, 0:2], 48 + 2 * j, 2, NH + 2 + j)

            def ffn(L):
                ffn_step(L, 0)
                ffn_step(L, 1)
                with dve.Fori(2, FJ) as j:
                    ffn_step(L, j)
                add_down_last(L)

            ffn(0)
            dve.wait_ge(ada_added, NH + 1 + FJ)
            coefs(2, 1, 0)
            coefs(3, 1, 1)
            gates(2, 1, 0)
            gates(3, 1, 1).then_inc(coef_ready, 1)
            dve.wait_ge(coef_ready, 3)
            next_stream(3, 1, True, False)
            for t in range(4):
                pool_tile(dve, "v", t)
                if t:
                    lo_of_diff(dve, "v", t - 1)
            lo_of_diff(dve, "v", 3)
            even_sums(5, 0)
            next_stream(5, 2, False, True)
            ffn(1)
            for h in range(2):
                norm_diagonal(7, h)
                gate_tiles(3, 7, h, range(KT))


def kernel(**inputs):
    import numpy as np
    import concourse.bacc as bacc
    from concourse.bass_utils import run_bass_kernel_spmd as run

    a = {k: np.asarray(v) for k, v in inputs.items()}

    def channel_major(x):
        return np.ascontiguousarray(x.reshape(x.shape[0], -1, P).transpose(2, 1, 0))

    def columns(v):
        return v.reshape(-1, P).T

    def out_tiles(w):
        return w.reshape(KT, P, -1, P).transpose(2, 1, 0, 3).reshape(-1, P, D)

    par = np.concatenate([columns(a[n]) for n in (
        "ada_b", "norm_pre_mix", "norm_post_mix", "norm_pre_ffn", "norm_post_ffn", "rg_conv_w", "rg_conv_b",
        "rg_gate_a_b", "rg_gate_x_b", "rg_lambda", "pool_b", "pool_scale", "ffn_conv_w", "ffn_conv_b")]
        + [np.stack([columns(a["c"]), columns(a["c_ctx"])], axis=-1).reshape(P, 16)], axis=1)
    w_in, w_out = out_tiles(a["rg_w_in"][0]), out_tiles(a["rg_w_out"][0])
    up = [out_tiles(a["ffn_w_up"][i]) for i in range(2)]
    down = a["ffn_w_down"].reshape(2 * FJ, P, D)
    pool = a["pool_w"][0].reshape(2, 2, 2, P, 256).transpose(0, 3, 1, 2, 4).reshape(2, P, D)
    slot_a = np.concatenate([w_in[NH:], w_out[0::2], up[0][:FJ], pool[0:1], up[1][:FJ]])
    slot_b = np.concatenate([w_in[:NH], w_out[1::2], up[0][FJ:], pool[1:2], up[1][FJ:]])
    gw = np.stack([a["rg_gate_a_w"][0], a["rg_gate_x_w"][0]], axis=1)
    gw = gw.transpose(2, 3, 0, 1, 4).reshape(NH, P, 4, P)
    ada = np.concatenate([out_tiles(a["ada_w"][i]) for i in range(2)])

    def reach(n, w):
        t = np.arange(n)
        return np.clip(t + w // 2, 0, n) - np.clip(t - w // 2, 0, n)

    cnt = np.stack([(1.0 / np.outer(reach(GR, w), reach(GW, w))).reshape(T) for w in WINDOWS]).astype(np.float32)
    arrays = {
        "xT": channel_major(a["x"][0]), "ctxT": channel_major(a["ctx"][0]), "params": par, "ada": ada,
        "wA": slot_a, "wB": slot_b, "wC": down, "gatew": gw, "poolcnt": cnt,
        "ident_in": np.eye(P, dtype=np.float32),
    }
    arrays = {k: np.ascontiguousarray(v) for k, v in arrays.items()}
    nc = bacc.Bacc("TRN2", target_bir_lowering=False, num_devices=1, dynamic_dma_scratch_size=1024)
    aps = [nc.dram_tensor(k, v.shape, F32, kind="ExternalInput").ap() for k, v in arrays.items()]
    out = nc.dram_tensor("outT", (P, KT, T), F32, kind="ExternalOutput").ap()
    build_trunk(nc, *aps, out)
    r = run(nc, [arrays], core_ids=[0])
    return r.results[0]["outT"].transpose(2, 1, 0).reshape(1, T, D)
```

```python
from contextlib import ExitStack

import concourse.bass as bass
from concourse import mybir

P = 128
D = 1024
T = 1024
NC_ = 256
KT = D // P
HF = 512
NH = 8
FJ = 3 * D // P
GW = 64
GR = T // GW
WINDOWS = (2, 4, 8, 16)
EPS = 1e-6
RG_C = 8.0

LAT = NC_ + 2
TA = LAT + T

_COLS = {}
_at = 0
for _name, _n in (("ada_b", 96), ("npre_mix", 16), ("npost_mix", 16), ("npre_ffn", 16), ("npost_ffn", 16),
                  ("rg_conv_w", 32), ("rg_conv_b", 8), ("gate_a_b", 16), ("gate_x_b", 16), ("lam", 16),
                  ("pool_b", 8), ("pool_scale", 8), ("ffn_conv_w", 144), ("ffn_conv_b", 48), ("cond", 16)):
    _COLS[_name] = _at
    _at += _n
NPAR = _at

ADA0 = 16
N_FFN = (NH + 4, NH + 4 + FJ)
N_AB = N_FFN[1] + FJ

F32 = mybir.dt.float32
F32R = mybir.dt.float32r
ALU = mybir.AluOpType
ACT = mybir.ActivationFunctionType


def build_trunk(nc, xT, ctxT, params, ada, wA, wB, wC, gatew, poolw, poolcnt, ident_in, outT):
    with ExitStack() as top:
        def sb(name, shape, dt=F32, scope=top):
            return scope.enter_context(nc.sbuf_tensor(name, shape, dt))

        def sem(name):
            return top.enter_context(nc.semaphore(name))

        Y = sb("Y", [P, KT, T])
        slots = ("A", "B", "C")
        raw = {s: sb(f"raw{s}", [P, D]) for s in slots}
        W_hi = {s: sb(f"W{s}_hi", [P, D], F32R) for s in slots}
        W_lo = {s: sb(f"W{s}_lo", [P, D], F32R) for s in slots}
        S = [sb(f"S{i}", [P, T]) for i in range(2)]
        par = sb("par", [P, NPAR])
        M = sb("M", [P, 96])
        Mc = sb("Mc", [P, ADA0])
        silu_c = sb("silu_c", [P, KT, 2])
        cA = sb("cA", [P, 4, KT])
        cAc = sb("cAc", [P, KT])
        cG = sb("cG", [P, 4, KT])
        pbs = sb("pbs", [P, KT])
        ident = sb("ident", [P, P])
        ones = sb("ones", [P, P])
        eps = sb("eps", [P, 1])
        rms = sb("rms", [P, KT])
        rstd = sb("rstd", [P, KT])
        rms_c = sb("rms_c", [P, 2])
        rstd_c = sb("rstd_c", [P, 2])
        sp = sb("sp", [P, 8, 2 * NH])
        s_tanh = sb("s_tanh", [P, 2 * NH])
        s_exp = sb("s_exp", [P, 2 * NH])

        def overlay(*plan):
            with ExitStack() as scope:
                out = []
                for n, item in enumerate(plan):
                    if isinstance(item, tuple):
                        out.append(sb(*item, scope=scope))
                    else:
                        sb(f"gap_{plan[-1][0]}_{n}", [P, int(item * 256)], scope=scope)
            return out

        H_hi, H_lo = overlay(("H_hi", [P, KT, T], F32R), ("H_lo", [P, KT, T], F32R))
        ada_first, ctx_x, ctx_sq, diag_c = overlay(
            ("ada_first", [P, ADA0, D]), ("ctx_x", [P, KT, NC_]), ("ctx_sq", [P, KT, NC_]), ("diag_c", [P, 2, P]))
        rec, u, RA0, Hc_hi, Hc_lo, RA1, IB0, IB1, TH0, TH1, gw = overlay(
            64, ("rec", [P, TA + 3]), ("u", [P, TA]), ("RA0", [P, TA]), 1.25,
            ("Hc_hi", [P, KT, NC_], F32R), ("Hc_lo", [P, KT, NC_], F32R), ("RA1", [P, TA]),
            ("IB0", [P, TA]), ("IB1", [P, TA]), ("TH0", [P, TA]), ("TH1", [P, TA]), ("gw", [P, 4, P]))
        RA, IB, TH = (RA0, RA1), (IB0, IB1), (TH0, TH1)
        E0, E1, red = overlay(
            124, ("E0", [P, KT, P]), ("E1", [P, KT, P]), ("red", [P, 4, P]))
        E = (E0, E1)
        ada_part, = overlay(124, ("ada_part", [P, 2, KT, P]))
        X, Ub, acc0, acc1, diag, F_hi, F_lo = overlay(
            64, ("X", [P, KT, T]), ("Ub", [P, T + 2]), ("acc0", [P, T]), ("acc1", [P, T]),
            ("diag", [P, KT, P]), ("F_hi", [P, T], F32R), ("F_lo", [P, T], F32R))
        acc = (acc0, acc1)
        Pf, pool_w, neg_w = overlay(
            ("Pf", [P, KT, T]), ("pool_w", [P, 2, D]), ("neg_w", [P, 2, D // 2]))
        col_v, row_v, pt0, pt1, col_p, row_p, pt_p = overlay(
            96, ("col_v", [P, GR, GW + 16]), ("row_v", [P, GR + 16, GW]),
            ("pt0", [P, (GR + 14) * GW]), ("pt1", [P, (GR + 14) * GW]),
            ("col_p", [P, GR, GW + 4]), ("row_p", [P, GR + 4, GW]), ("pt_p", [P, (GR + 3) * GW]))
        ps = top.enter_context(nc.psum_tensor("ps", [P, 8, 512], F32))
        AB01, AB23, AB45, AB67 = (ps[:, b:b + 2, :] for b in (0, 2, 4, 6))

        par_full, ctx_full, const_full = sem("par_full"), sem("ctx_full"), sem("const_full")
        x_full = [sem(f"x_full{q}") for q in range(4)]
        res_full = [sem(f"res_full{q}") for q in range(4)]
        ada_first_full = [sem(f"ada_first_full{q}") for q in range(4)]
        e_full = [sem(f"ada_full{i}") for i in range(2)]
        raw_full = {s: sem(f"raw_full_{s}") for s in slots}
        w_hi = {s: sem(f"w_hi_{s}") for s in slots}
        w_ready = {s: sem(f"w_ready_{s}") for s in slots}
        unit_done = {s: sem(f"unit_done_{s}") for s in "AB"}
        gw_full, gate_done, gate_evac = sem("gw_full"), sem("gate_done"), sem("gate_evac")
        memset_done, zeros_ready = sem("memset_done"), sem("zeros_ready")
        silu_done, softplus_step, lam_ready = sem("silu_done"), sem("softplus_step"), sem("lam_ready")
        part_step = sem("ada_part_step")
        e_mul, red_made = sem("ada_mul"), sem("ada_red_made")
        ada_out, ada_added, coef_ready = sem("ada_out"), sem("ada_added"), sem("coef_ready")
        sq_made, sum_even, sum_odd, sum_both = sem("sq_made"), sem("sum_even"), sem("sum_odd"), sem("sum_both")
        sum_last = sem("sum_last")
        ssq_done, rms_made, rstd_made = sem("ssq_done"), sem("rms_made"), sem("rstd_made")
        diag_made, rb_done = sem("diag_made"), sem("rb_done")
        csq_made, cssq_done, crms_made = sem("ctx_sq_made"), sem("ctx_ssq_done"), sem("ctx_rms_made")
        crstd_made, cdiag_made, crb_done = sem("ctx_rstd_made"), sem("ctx_diag_made"), sem("ctx_rb_done")
        cscaled, caffine, chi, hc_ready = sem("ctx_scaled"), sem("ctx_affine"), sem("ctx_hi"), sem("ctx_h_ready")
        x_scaled, affine_made, h_hi = sem("x_scaled"), sem("affine_made"), sem("h_hi")
        h_ready = (sem("h_ready_even"), sem("h_ready_odd"))
        gated_ready = (sem("gated_ready_even"), sem("gated_ready_odd"))
        y_scaled, y_evac = sem("y_scaled"), sem("y_evac")
        x_new = (sem("x_new_even"), sem("x_new_odd"))
        rec_evac, conv_step, u_made = sem("rec_evac"), sem("conv_step"), sem("u_made")
        g_made, tanh_made, exp_made, sqrt_made = sem("g_made"), sem("tanh_made"), sem("exp_made"), sem("sqrt_made")
        mult_made, iu_made, b_made = sem("mult_made"), sem("iu_made"), sem("b_made")
        scan_ctx, scan_done, ysum_made, gy_made = sem("scan_ctx"), sem("scan_done"), sem("ysum_made"), sem("gy_made")
        u_evac, tap_done, conv_a, conv_done = sem("u_evac"), sem("tap_done"), sem("conv_a"), sem("conv_done")
        gelu_done, f_mul, f_hi, f_ready = sem("gelu_done"), sem("f_mul"), sem("f_hi"), sem("f_ready")
        d_done, d_added = sem("d_done"), sem("d_added")
        pads_ready, tile_affine = sem("pads_ready"), sem("tile_affine")
        col_loaded = {e: sem(f"col_loaded_{e}") for e in "vp"}
        pool_step = {e: sem(f"pool_step_{e}") for e in "vp"}
        pooled = {e: sem(f"pooled_{e}") for e in "vp"}
        last_mul, last_hi, last_ready = sem("last_f_mul"), sem("last_f_hi"), sem("last_f_ready")
        cnt_full = {e: sem(f"cnt_full_{e}") for e in "vp"}
        poolw_full, neg_ready, pool_mm, out_done = sem("poolw_full"), sem("neg_ready"), sem("pool_mm"), sem("out_done")

        block = top.enter_context(nc.Block())

        def col(name, n=0, w=1):
            c = _COLS[name] + n
            return par[:, bass.ds(c, w)]

        def flat(banks):
            return banks.rearrange("p a b -> p (a b)")

        def hs(h):
            return slice(h * HF, h * HF + HF)

        H_BASE = {0: 0, 1: 16, 2: 24, 4: 40}
        FILL = {0: 0, 1: 2, 3: 4}
        AFFINE_BASE = {0: 0, 1: 8, 3: 16}
        POOL_TILES = {"p": (0, 1, 2, 3), "v": (4, 5, 6, 7)}
        POOL_GROUPS = (0, 2, 3, 1)
        LATE = POOL_GROUPS[2:]
        POOL_OUT = tuple(2 * g + m for g in POOL_GROUPS for m in range(2))

        def last_sums(dve, n, cols, count):
            dve.wait_ge(sum_even, 3 * n + 3 * count)
            dve.wait_ge(sum_odd, 2 * n + 2 * count)
            dve.tensor_tensor(acc[0][:, cols], acc[0][:, cols], acc[1][:, cols], ALU.add).then_inc(sum_both, count)
            dve.wait_ge(sum_both, n + count)
            dve.wait_ge(sq_made, 8 * n + 8 * count)
            dve.tensor_tensor(acc[0][:, cols], acc[0][:, cols], S[1][:, cols], ALU.add).then_inc(sum_last, count)

        def ssq_bank(q, h):
            return 2 if q in (3, 7) else 4 + h

        def rb_bank(q, h):
            return 3 if q in (3, 7) and h == 0 else 6 + h

        def wait_h(eng, fill, h, k):
            eng.wait_ge(h_ready[k % 2], 8 * (fill // 2) + 4 * h + k // 2 + 1)

        def window_stages(w):
            return w.bit_length() - 1

        def pool_steps(e, t):
            return sum(2 * window_stages(WINDOWS[k // 2]) + (k // 2 in LATE) for k in POOL_TILES[e][:t])

        def wait_new(eng, i, h, m):
            eng.wait_ge(x_new[m % 2], 8 * i + 4 * h + m // 2 + 1)

        @block.sync
        def _(sp_):
            def load_raw(s, n):
                if not (isinstance(n, int) and n == 0):
                    sp_.wait_ge(w_ready[s], n)
                sp_.dma_start(raw[s][:], {"A": wA, "B": wB, "C": wC}[s][n]).then_inc(raw_full[s], 16)

            def load_pair(p):
                if not (isinstance(p, int) and p == 0):
                    sp_.wait_ge(red_made, 2 * p)
                for i in range(2):
                    sp_.dma_start(E[i][:], ada[ADA0 + 2 * p + i].rearrange("p (k m) -> p k m", k=KT))\
                       .then_inc(e_full[i], 16)

            def load_first(q):
                sp_.dma_start(ada_first[:, 4 * q:4 * q + 4], ada[4 * q:4 * q + 4].rearrange("u p c -> p u c"))\
                   .then_inc(ada_first_full[q], 16)

            def load_x(q, dst, full):
                sp_.dma_start(dst[:, 2 * q:2 * q + 2], xT[:, 2 * q:2 * q + 2]).then_inc(full[q], 16)

            sp_.dma_start(par[:], params).then_inc(par_full, 16)
            sp_.dma_start(ctx_x[:], ctxT).then_inc(ctx_full, 16)
            sp_.dma_start(ident[:], ident_in).then_inc(const_full, 16)
            for q in range(4):
                load_first(q)
            for q in range(4):
                load_x(q, Y, x_full)
            load_raw("A", 0)
            load_raw("B", 0)
            sp_.dma_start(gw[:], gatew[0]).then_inc(gw_full, 16)
            load_raw("A", 1)
            load_raw("B", 1)
            sp_.wait_ge(ada_out, 1)
            load_pair(0)

            def head_loads(hd, last=False):
                load_raw("A", hd + 2)
                load_pair(2 * hd + 1)
                load_raw("B", hd + 2)
                if not last:
                    sp_.wait_ge(gate_done, 4 * hd + 4)
                    sp_.dma_start(gw[:], gatew[hd + 1]).then_inc(gw_full, 16)
                load_pair(2 * hd + 2)

            head_loads(0)
            with sp_.Fori(1, NH - 1) as hd:
                head_loads(hd)
            head_loads(NH - 1, last=True)
            sp_.wait_ge(gy_made, NH)
            for i in range(4):
                load_x(i, X, res_full)
                if i == 1:
                    load_raw("C", 0)
                load_raw("A", NH + 2 + i)
                load_raw("B", NH + 2 + i)

            def ffn_loads(L, j):
                n, c = N_FFN[L] + j, FJ * L + j
                static = isinstance(j, int)
                more = not static or j < FJ - 1 and n + 2 < N_AB
                if more:
                    load_raw("A", n + 2)
                if L == 0 and not (static and j == FJ - 1):
                    load_pair(2 * NH + j + 1)
                if not static or c + 1 < 2 * FJ:
                    load_raw("C", c + 1)
                if more:
                    load_raw("B", n + 2)

            def ffn(L):
                ffn_loads(L, 0)
                with sp_.Fori(1, FJ - 2) as j:
                    ffn_loads(L, j)
                ffn_loads(L, FJ - 2)
                ffn_loads(L, FJ - 1)

            ffn(0)
            sp_.wait_ge(unit_done["B"], N_FFN[1])
            sp_.dma_start(pool_w[:], poolw.rearrange("u p c -> p u c")).then_inc(poolw_full, 16)
            sp_.wait_ge(ssq_done, 10)
            for i, (e, g) in enumerate((("p", 0), ("v", 2), ("p", 1), ("v", 3))):
                if i >= 2:
                    sp_.wait_ge(pooled[e], 2)
                sp_.dma_start(S["pv".index(e)][:], poolcnt[g:g + 1, :].to_broadcast([P, T]))\
                   .then_inc(cnt_full[e], 16)
            load_raw("A", N_FFN[1] + 1)
            load_raw("B", N_FFN[1] + 1)
            ffn(1)
            for h in range(2):
                for m in range(KT):
                    wait_new(sp_, 3, h, m)
                    sp_.dma_start(outT[:, m, hs(h)], X[:, m, hs(h)]).then_inc(out_done, 16)
            sp_.wait_ge(out_done, 16 * 2 * KT)

        @block.tensor
        def _(pe):
            def product(s, w_cols, pieces, first=True, last=True):
                for w, part in ((W_hi[s], 0), (W_hi[s], 1), (W_lo[s], 0)):
                    for out, hi, lo in pieces:
                        mm = pe.matmul(out, w[:, w_cols:w_cols + P], (hi, lo)[part],
                                       start=first and w is W_hi[s] and part == 0,
                                       stop=last and w is W_lo[s])
                return mm

            def piece(banks, hi, lo, k, h):
                return banks[:, h], hi[:, k, hs(h)], lo[:, k, hs(h)]

            def unit(s, n, banks):
                pe.wait_ge(w_ready[s], n + 1)
                for k in range(KT):
                    mm = product(s, k * P, [piece(banks, H_hi, H_lo, k, h) for h in range(2)], k == 0, k == KT - 1)
                mm.then_inc(unit_done[s], 1)

            def first_units(fill, units, h, context=None):
                for s, n, banks in units:
                    pe.wait_ge(w_ready[s], n + 1)
                    for k in range(KT):
                        wait_h(pe, fill, h, k)
                        pieces = [piece(banks, H_hi, H_lo, k, h)]
                        if context is not None and h == 1 and s == "A":
                            pe.wait_ge(hc_ready, 1)
                            pieces.append((context, Hc_hi[:, k], Hc_lo[:, k]))
                        mm = product(s, k * P, pieces, k == 0, k == KT - 1)
                    if h == 1:
                        mm.then_inc(unit_done[s], 1)

            def ada_columns(n_red, n, out):
                pe.wait_ge(red_made, n_red)
                for i in range(n):
                    mm = pe.matmul(out[:, i:i + 1], red[:, i], ones[:, 0:1], start=True, stop=True)
                mm.then_inc(ada_out, 1)

            def square_sums(q, h):
                n = 2 * q + h
                pe.wait_ge(sum_last, n + 1)
                for t in range(4):
                    c = h * HF + t * P
                    mm = pe.matmul(ps[:, ssq_bank(q, h), 4 * h + t:4 * h + t + 1], acc[0][:, c:c + P], ones[:, 0:1],
                                   start=True, stop=True)
                mm.then_inc(ssq_done, 1)

            def spread(q, h):
                pe.wait_ge(diag_made, 2 * q + h + 1)
                pe.matmul(ps[:, rb_bank(q, h)], ones[:], diag[:, 4 * h:4 * h + 4], start=True, stop=True)\
                    .then_inc(rb_done, 1)

            def norm(q, h):
                square_sums(q, h)
                spread(q, h)

            pe.wait_ge(memset_done, 3)
            pe.wait_ge(csq_made, 1)
            for t in range(2):
                for k in range(KT):
                    mm = pe.matmul(ps[:, 0, t:t + 1], ctx_sq[:, k, t * P:(t + 1) * P], ones[:, 0:1],
                                   start=k == 0, stop=k == KT - 1)
            mm.then_inc(cssq_done, 1)
            pe.wait_ge(silu_done, 1)
            for q in (0, 2):
                pe.wait_ge(ada_first_full[q], 16)
                for n in range(4 * q, 4 * q + 4):
                    for k in range(KT):
                        pe.matmul(ps[:, 2, 2 * n:2 * n + 2], ada_first[:, n, k * P:k * P + P], silu_c[:, k],
                                  start=k == 0, stop=k == KT - 1)
                if q == 0:
                    pe.wait_ge(cdiag_made, 1)
                    pe.matmul(ps[:, 3, 0:NC_], ones[:], diag_c[:], start=True, stop=True).then_inc(crb_done, 1)
            for q in (1, 3):
                pe.wait_ge(part_step, 8 * (q + 1))
                for n in range(4):
                    for v in range(2):
                        c = 2 * (4 * q + n) + v
                        mm = pe.matmul(ps[:, 2, c:c + 1], ada_part[:, v, 4 * (q // 2) + n], ones[:, 0:1],
                                       start=True, stop=True)
            mm.then_inc(ada_out, 1)
            norm(0, 0)
            norm(0, 1)

            def head(hd, last=False):
                if not (isinstance(hd, int) and hd == 0):
                    pe.wait_ge(gate_evac, 4 * hd)
                    ada_columns(4 * hd, 4, ps[:, 3, 0:4])
                    pe.wait_ge(g_made, hd)
                    unit("B", hd, AB67)
                pe.wait_ge(gw_full, 16 * hd + 16)
                pe.wait_ge(u_made, hd + 1)
                for gi in range(4):
                    if gi == 0:
                        pe.wait_ge(rec_evac, hd + 1)
                    elif gi == 1:
                        pe.wait_ge(ada_added, hd + 1)
                    else:
                        pe.wait_ge(gate_evac, 4 * hd + gi - 1)
                    b = 3 * (gi % 2)
                    for out, src in ((ps[:, b, 0:NC_], u[:, 0:NC_]), (ps[:, b + 1], u[:, LAT:LAT + HF]),
                                     (ps[:, b + 2], u[:, LAT + HF:TA])):
                        mm = pe.matmul(out, gw[:, gi], src, start=True, stop=True)
                    mm.then_inc(gate_done, 1)
                if not last:
                    pe.wait_ge(gate_evac, 4 * hd + 3)
                    s, n = "A", hd + 1
                    pe.wait_ge(w_ready[s], n + 1)
                    for k in range(KT):
                        pieces = [piece(ps[:, 1:3, :], H_hi, H_lo, k, h) for h in range(2)]
                        pieces.append((ps[:, 0, 0:NC_], Hc_hi[:, k], Hc_lo[:, k]))
                        mm = product(s, k * P, pieces, k == 0, k == KT - 1)
                    mm.then_inc(unit_done[s], 1)

            pe.wait_ge(ada_added, 1)
            for h in range(2):
                first_units(0, (("A", 0, ps[:, 1:3, :]), ("B", 0, AB67)), h, context=ps[:, 0, 0:NC_])
            head(0)
            with pe.Fori(1, NH - 1) as hd:
                head(hd)
            head(NH - 1, last=True)

            pe.wait_ge(gate_evac, 4 * NH)
            for k in range(KT):
                pe.wait_ge(gated_ready[k % 2], k // 2 + 1)
                for s, banks in (("A", AB01), ("B", AB23)):
                    if k == 0:
                        pe.wait_ge(w_ready[s], NH + 1)
                    mm = product(s, k * P, [piece(banks, H_hi, H_lo, k, h) for h in range(2)], k == 0, k == KT - 1)
                    if k == KT - 1:
                        mm.then_inc(unit_done[s], 1)

            def out_pair(i):
                pe.wait_ge(y_evac, 2 * i - 1)
                unit("A", NH + i, AB01)
                pe.wait_ge(y_evac, 2 * i)
                unit("B", NH + i, AB23)

            out_pair(1)
            ada_columns(4 * NH, 4, ps[:, 4, 0:4])
            with pe.Fori(2, 4) as i:
                out_pair(i)
            pe.wait_ge(ada_added, NH + 1)
            norm(1, 0)
            norm(1, 1)

            def down(L, j):
                c = FJ * L + j
                pe.wait_ge(w_ready["C"], c + 1)
                pe.wait_ge(f_ready, c + 1 - L)
                for m in range(KT):
                    if m < 2:
                        if not (isinstance(c, int) and c == 0):
                            pe.wait_ge(d_added, 8 * c)
                        if m == 0 and L == 0:
                            pe.wait_ge(ada_added, NH + 2 + j)
                    elif m == 2:
                        pe.wait_ge(u_evac, c + 2)
                    else:
                        pe.wait_ge(d_added, 8 * c + m - 2)
                    b = (4, 6, 0)[m % 3]
                    product("C", m * P, [(ps[:, b + h], F_hi[:, hs(h)], F_lo[:, hs(h)]) for h in range(2)])\
                        .then_inc(d_done, 1)

            def down_last(L):
                c = FJ * (L + 1) - 1
                q = 3 + 4 * L
                bank = (6, 7, 0, 1, 4, 5)

                def half_tile(n, last):
                    h, m = divmod(n, KT)
                    s, hi, lo = ("B", W_hi["A"], W_lo["A"]) if last else ("C", F_hi, F_lo)
                    return product(s, m * P, [(ps[:, bank[n % 6]], hi[:, hs(h)], lo[:, hs(h)])], not last, last)

                pe.wait_ge(w_ready["C"], c)
                pe.wait_ge(f_ready, c - L)
                pe.wait_ge(d_added, 8 * (c - 1))
                pe.wait_ge(u_evac, c + 1)
                for n in range(6):
                    if n == 4 and L == 0:
                        pe.wait_ge(ada_added, NH + 1 + FJ)
                    half_tile(n, False)
                pe.wait_ge(w_ready["C"], c + 1)
                pe.wait_ge(last_ready, 2 * L + 1)
                for n in range(6):
                    half_tile(n, True).then_inc(d_done, 1)
                for n in range(6, 2 * KT):
                    if n == KT:
                        pe.wait_ge(last_ready, 2 * L + 2)
                    pe.wait_ge(d_added, 8 * (c - 1) + n - 5)
                    half_tile(n, False)
                    half_tile(n, True).then_inc(d_done, 1)
                    if n == 10:
                        square_sums(q, 0)
                    if n == 13:
                        spread(q, 0)
                norm(q, 1)

            def ffn_step(L, j):
                n, c = N_FFN[L] + j, FJ * L + j
                static = isinstance(j, int)
                last = static and j == FJ - 1
                if not (static and j == 0):
                    pe.wait_ge(u_evac, c)
                    if not (static and j == 1):
                        pe.wait_ge(d_added, 8 * c - 10)
                    unit("A", n, AB01)
                    if static and j == 1 and L == 0:
                        ada_columns(4 * NH + 2, 2, ps[:, 4, 0:2])
                    if not last:
                        down(L, j - 1)
                    pe.wait_ge(f_mul, c - L)
                    unit("B", n, AB23)
                if L == 0 and not (static and j == 0):
                    pe.wait_ge(d_added, 8 * (j - 1 if last else j) - 1)
                    ada_columns(4 * NH + 2 * j + 2, 2, ps[:, 4, 0:2])

            def ffn(L):
                for h in range(2):
                    norm(2 + 4 * L, h)
                    first_units(2 + 2 * L, (("A", N_FFN[L], AB01), ("B", N_FFN[L], AB23)), h)
                ffn_step(L, 0)
                ffn_step(L, 1)
                with pe.Fori(2, FJ - 1) as j:
                    ffn_step(L, j)
                ffn_step(L, FJ - 1)
                down_last(L)

            ffn(0)
            norm(4, 0)
            norm(4, 1)

            pe.wait_ge(poolw_full, 16)
            pe.wait_ge(neg_ready, 1)
            pe.wait_ge(tile_affine, KT)
            for at, g in enumerate(POOL_GROUPS):
                if at >= 2:
                    pe.wait_ge(y_evac, 8 + 2 * at - 2)
                late = g in LATE
                for part in range(int(late), 2):
                    if part:
                        pe.wait_ge(pooled["pv"[g // 2]], 2 * (g % 2) + 2)
                    w, src = ((neg_w, Y), (pool_w, Pf))[part]
                    for m in range(2):
                        banks = ((AB01, AB23), (AB45, AB67))[at % 2][m]
                        for k in range(2):
                            c = (g % 2) * 512 + k * 256 + m * P
                            for h in range(2):
                                mm = pe.matmul(banks[:, h], w[:, g // 2, c:c + P], src[:, 2 * g + k, hs(h)],
                                               start=part == late and k == 0, stop=part == 1 and k == 1)
                        if part:
                            mm.then_inc(pool_mm, 1)
            norm(5, 0)
            norm(5, 1)
            ffn(1)

        @block.scalar
        def _(act):
            A = act.activation

            def round_hi(s, n):
                act.wait_ge(raw_full[s], 16 * n + 16)
                if not (isinstance(n, int) and n == 0):
                    act.wait_ge(unit_done[s], n)
                A(W_hi[s][:], raw[s][:], ACT.Copy).then_inc(w_hi[s], 1)

            def round_down(L, j):
                c = FJ * L + j
                act.wait_ge(raw_full["C"], 16 * c + 16)
                if not (isinstance(c, int) and c == 0):
                    act.wait_ge(d_done, 8 * c)
                A(W_hi["C"][:], raw["C"][:], ACT.Copy).then_inc(w_hi["C"], 1)

            def square(q, h, p, src):
                n = 2 * q + h
                if p < 2:
                    dst = acc[p]
                    if q:
                        act.wait_ge(ssq_done, n - 1)
                else:
                    dst = S[p % 2]
                    if p >= 4:
                        act.wait_ge((sum_even, sum_odd)[p % 2], (3, 2)[p % 2] * n + p // 2 - 1)
                A(dst[:, hs(h)], src[:, hs(h)], ACT.Square).then_inc(sq_made, 1)

            def square_whole(q, p, src):
                if p < 2:
                    dst = acc[p]
                    act.wait_ge(ssq_done, 2 * q)
                else:
                    dst = S[p % 2]
                    if p >= 4:
                        act.wait_ge((sum_even, sum_odd)[p % 2], (6, 4)[p % 2] * q + 2 * (p // 2 - 1))
                A(dst[:], src, ACT.Square).then_inc(sq_made, 2)

            def norm_root(q, h):
                act.wait_ge(ssq_done, 2 * q + h + 1)
                A(rms[:, 4 * h:4 * h + 4], ps[:, ssq_bank(q, h), 4 * h:4 * h + 4], ACT.Sqrt, scale=1.0 / D,
                  bias=eps[:, 0:1]).then_inc(rms_made, 1)

            def fill_h(i, L, ffn_part, h):
                for k in range(KT):
                    act.wait_ge(x_scaled, 16 * i + 8 * h + k + 1)
                    c = 48 * L + 24 * ffn_part + k
                    if k % 2 == 0:
                        A(H_hi[:, k, hs(h)], Y[:, k, hs(h)], ACT.Identity, bias=M[:, c:c + 1]).then_inc(h_hi, 1)
                    else:
                        A(Y[:, k, hs(h)], Y[:, k, hs(h)], ACT.Identity, bias=M[:, c:c + 1]).then_inc(affine_made, 1)
                        act.wait_ge(affine_made, AFFINE_BASE[i] + 4 * h + k // 2 + 1)
                        A(H_hi[:, k, hs(h)], Y[:, k, hs(h)], ACT.Copy).then_inc(h_hi, 1)

            act.wait_ge(par_full, 16)
            A(silu_c[:], col("cond", 0, 16).rearrange("p (k v) -> p k v", v=2), ACT.Silu).then_inc(silu_done, 1)
            A(sp[:, 0], col("lam", 0, 16), ACT.Abs).then_inc(softplus_step, 1)
            act.wait_ge(softplus_step, 1)
            A(sp[:, 1], sp[:, 0], ACT.Exp, scale=-1.0).then_inc(softplus_step, 1)
            act.wait_ge(softplus_step, 3)
            A(sp[:, 3], sp[:, 2], ACT.Ln).then_inc(softplus_step, 1)
            act.wait_ge(ctx_full, 16)
            A(ctx_sq[:], ctx_x[:], ACT.Square).then_inc(csq_made, 1)
            act.wait_ge(memset_done, 3)
            act.wait_ge(cssq_done, 1)
            A(rms_c[:], ps[:, 0, 0:2], ACT.Sqrt, scale=1.0 / D, bias=eps[:, 0:1]).then_inc(crms_made, 1)
            for h in range(2):
                for m in range(KT):
                    act.wait_ge(x_full[m // 2], 16)
                    square(0, h, m, Y[:, m])
            round_hi("A", 0)
            norm_root(0, 0)
            round_hi("B", 0)
            norm_root(0, 1)
            act.wait_ge(caffine, KT)
            A(Hc_hi[:], ctx_x[:], ACT.Copy).then_inc(chi, 1)
            act.wait_ge(coef_ready, 1)
            for h in range(2):
                fill_h(0, 0, 0, h)

            def gated_hi(k):
                act.wait_ge(gy_made, k + 1)
                A(H_hi[:, k], Y[:, k], ACT.Copy).then_inc(h_hi, 1)

            def head(hd, last=False):
                first = isinstance(hd, int) and hd == 0
                act.wait_ge(unit_done["A"], hd + 1)
                if not first:
                    act.wait_ge(u_made, hd)
                A(rec[:, 2:2 + NC_], ps[:, 0, 0:NC_], ACT.Copy)
                A(rec[:, 2 + LAT:2 + TA], flat(ps[:, 1:3, :]), ACT.Copy).then_inc(rec_evac, 1)
                round_hi("A", hd + 1)
                act.wait_ge(unit_done["B"], hd + 1)
                A(Y[:, hd], flat(AB67), ACT.Gelu_apprx_tanh).then_inc(g_made, 1)
                for gi in range(4):
                    d, b = gi // 2, 3 * (gi % 2)
                    dst, name = ((RA[d], "gate_a_b"), (IB[d], "gate_x_b"))[gi % 2]
                    act.wait_ge(gate_done, 4 * hd + gi + 1)
                    if not first:
                        act.wait_ge(scan_done, 2 * hd - 1 + d)
                    A(dst[:, 0:NC_], ps[:, b, 0:NC_], ACT.Sigmoid, bias=col(name, d * NH + hd))
                    A(dst[:, LAT:TA], flat(ps[:, b + 1:b + 3, :]), ACT.Sigmoid, bias=col(name, d * NH + hd))\
                        .then_inc(gate_evac, 1)
                round_hi("B", hd + 1)
                for d in range(2):
                    act.wait_ge(gate_evac, 4 * hd + 2 * d + 2)
                    if not first:
                        act.wait_ge(gy_made, hd)
                    A(TH[d][:], RA[d][:], ACT.Tanh, scale=s_tanh[:, bass.ds(d * NH + hd, 1)])\
                        .then_inc(tanh_made, 1)
                if last:
                    gated_hi(0)
                    gated_hi(1)
                for d in range(2):
                    A(RA[d][:], RA[d][:], ACT.Exp, scale=s_exp[:, bass.ds(d * NH + hd, 1)]).then_inc(exp_made, 1)
                if last:
                    gated_hi(2)
                for d in range(2):
                    act.wait_ge(tanh_made, 2 * hd + d + 1)
                    A(TH[d][:], TH[d][:], ACT.Sqrt).then_inc(sqrt_made, 1)

            act.wait_ge(lam_ready, 1)
            act.wait_ge(zeros_ready, 1)
            head(0)
            with act.Fori(1, NH - 1) as hd:
                head(hd)
            head(NH - 1, last=True)
            for k in range(3, KT):
                gated_hi(k)
            for m in range(KT):
                s, n = "AB"[m % 2], NH + m // 2
                act.wait_ge(unit_done[s], n + 1)
                round_hi(s, n + 1)
                A(Y[:, m], flat((AB01, AB23)[m % 2]), ACT.Copy).then_inc(y_evac, 1)
                act.wait_ge(y_evac, m + 1)
                square_whole(1, m, Y[:, m])
            round_down(0, 0)

            def squares_x(q, i, h, ms):
                for m in ms:
                    wait_new(act, i, h, m)
                    square(q, h, m, X[:, m])

            def next_stream(q, i, fill):
                if q != 3:
                    norm_root(q, 0)
                squares_x(q + 1, i, 0, range(4))
                if q != 3:
                    norm_root(q, 1)
                squares_x(q + 1, i, 0, range(4, KT))
                norm_root(q + 1, 0)
                squares_x(q + 1, i, 1, range(4))
                if fill is not None:
                    fill(0)
                squares_x(q + 1, i, 1, range(4, KT))
                norm_root(q + 1, 1)
                if fill is not None:
                    fill(1)

            def fill_ffn(L, h):
                act.wait_ge(coef_ready, 2 + L)
                fill_h(1 + 2 * L, L, 1, h)

            def ffn_step(L, j):
                n, c = N_FFN[L] + j, FJ * L + j
                static = isinstance(j, int)
                last = static and j == FJ - 1
                act.wait_ge(unit_done["A"], n + 1)
                if static and j == 0:
                    round_hi("A", n + 1)
                if not (static and c == 0):
                    act.wait_ge(conv_done, c)
                A(Ub[:, 1:T + 1], flat(AB01), ACT.Copy).then_inc(u_evac, 1)
                act.wait_ge(u_evac, c + 1)
                if not (static and c == 0):
                    act.wait_ge(f_mul, c - L)
                A(S[0][:], Ub[:, 1:T + 1], ACT.Identity, scale=col("ffn_conv_w", 72 * L + 24 + j),
                  bias=col("ffn_conv_b", 24 * L + j)).then_inc(tap_done, 1)
                if not last and not (static and j == 0):
                    round_hi("A", n + 1)
                act.wait_ge(conv_done, c + 1)
                A(S[0][:], S[0][:], ACT.Gelu_apprx_tanh).then_inc(gelu_done, 1)
                if last:
                    act.wait_ge(unit_done["B"], n + 1)
                    act.wait_ge(raw_full["C"], 16 * c + 16)
                    A(W_hi["B"][:], raw["C"][:], ACT.Copy).then_inc(w_hi["C"], 1)
                    for h in range(2):
                        act.wait_ge(last_mul, 2 * L + h + 1)
                        A(W_hi["A"][:, hs(h)], S[1][:, hs(h)], ACT.Copy).then_inc(last_hi, 1)
                    return
                if not (static and c == 0):
                    round_down(L, j)
                act.wait_ge(f_mul, c + 1 - L)
                A(F_hi[:], S[1][:], ACT.Copy).then_inc(f_hi, 1)
                round_hi("B", n + 1)

            def ffn(L):
                q = 3 + 4 * L
                ffn_step(L, 0)
                with act.Fori(1, FJ - 1) as j:
                    ffn_step(L, j)
                ffn_step(L, FJ - 1)
                for n in range(2 * KT):
                    act.wait_ge(d_added, 8 * (FJ * (L + 1) - 2) + n + 1)
                    square(q, n // KT, n % KT, Y[:, n % KT])
                    if n == 11:
                        norm_root(q, 0)
                norm_root(q, 1)

            next_stream(1, 0, lambda h: fill_ffn(0, h))
            ffn(0)
            next_stream(3, 1, None)

            def load_col(e, t):
                k, pad = POOL_TILES[e][t], {"p": 2, "v": 8}[e]
                dst = {"p": col_p, "v": col_v}[e][:, :, pad:pad + GW]
                if t == 0:
                    A(dst, Y[:, k].rearrange("p (r c) -> p r c", c=GW), ACT.Identity, bias=M[:, 48 + k:49 + k])\
                        .then_inc(col_loaded[e], 1)
                else:
                    act.wait_ge(tile_affine, k + 1)
                    act.wait_ge(pool_step[e], pool_steps(e, t - 1) + 1)
                    A(dst, Y[:, k].rearrange("p (r c) -> p r c", c=GW), ACT.Copy).then_inc(col_loaded[e], 1)

            act.wait_ge(coef_ready, 3)
            act.wait_ge(pads_ready, 1)
            for e in "pv":
                act.wait_ge(x_scaled, 32 + 8 + POOL_TILES[e][0] + 1)
                load_col(e, 0)
            for k in range(KT):
                act.wait_ge(x_scaled, 32 + 8 + k + 1)
                A(Y[:, k], Y[:, k], ACT.Identity, bias=M[:, 48 + k:49 + k]).then_inc(tile_affine, 1)
            for e in "pv":
                load_col(e, 1)
            for s in "AB":
                act.wait_ge(d_done, 8 * FJ)
                round_hi(s, N_FFN[1])
            act.wait_ge(poolw_full, 16)
            A(neg_w[:], pool_w[:, :, 0:512], ACT.Copy, scale=-1.0).then_inc(neg_ready, 1)
            for t in range(2, 4):
                for e in "pv":
                    load_col(e, t)
            for p, mt in enumerate(POOL_OUT):
                act.wait_ge(pool_mm, p + 1)
                A(Y[:, mt], flat((AB01, AB23, AB45, AB67)[p % 4]), ACT.Identity, scale=col("pool_scale", mt),
                  bias=pbs[:, mt:mt + 1]).then_inc(y_evac, 1)
                if p < 3:
                    continue
                for e in "pv":
                    act.wait_ge(pooled[e], 4)
                for done in range(0 if p == 3 else p, p + 1):
                    act.wait_ge(y_evac, 8 + done + 1)
                    square_whole(5, done, Y[:, POOL_OUT[done]])
            next_stream(5, 2, lambda h: fill_ffn(1, h))
            ffn(1)

        def pool_tile(eng, e, t):
            k = POOL_TILES[e][t]
            w = WINDOWS[k // 2]
            pad, off, colg, row, pts, cnt = {
                "p": (2, 0, col_p, row_p, (pt_p, pt_p), S[0]), "v": (8, 1, col_v, row_v, (pt0, pt1), S[1])}[e]
            n = pool_steps(e, t)
            inner = row[:, pad:pad + GR, :]
            TT = eng.tensor_tensor
            eng.wait_ge(col_loaded[e], t + 1)
            if t:
                eng.wait_ge(pooled[e], t)
            src = colg
            for stage in range(window_stages(w)):
                s = 2 << stage
                lo, hi = pad - (w - s) // 2, pad + GW + (w - s) // 2
                left, right = (1, 0) if s == 2 else (s // 4, -(s // 4))
                if s == w:
                    nxt, dst = None, inner
                else:
                    nxt = pts[stage % 2][:, 0:GR * (GW + 2 * pad)].rearrange("p (r c) -> p r c", c=GW + 2 * pad)
                    dst = nxt[:, :, lo:hi]
                if n:
                    eng.wait_ge(pool_step[e], n)
                TT(dst, src[:, :, lo - left:hi - left], src[:, :, lo - right:hi - right], ALU.add)\
                    .then_inc(pool_step[e], 1)
                n += 1
                src = nxt
            src, at = row[:].rearrange("p r c -> p (r c)"), 0
            for stage in range(window_stages(w)):
                s = 2 << stage
                lo, hi = pad - (w - s) // 2, pad + GR + (w - s) // 2
                left, right = (1, 0) if s == 2 else (s // 4, -(s // 4))
                if s == w and s > 2:
                    nxt, nxt_at = row[:].rearrange("p r c -> p (r c)"), 0
                else:
                    nxt, nxt_at = pts[stage % 2][:], off
                eng.wait_ge(pool_step[e], n)
                TT(nxt[:, (lo - nxt_at) * GW:(hi - nxt_at) * GW],
                   src[:, (lo - left - at) * GW:(hi - left - at) * GW],
                   src[:, (lo - right - at) * GW:(hi - right - at) * GW], ALU.add).then_inc(pool_step[e], 1)
                n += 1
                src, at = nxt, nxt_at
            own = src[:, (pad - at) * GW:(pad + GR - at) * GW]
            eng.wait_ge(pool_step[e], n)
            eng.wait_ge(cnt_full[e], 16 * (t // 2 + 1))
            if k // 2 in LATE:
                TT(own, own, cnt[:], ALU.mult).then_inc(pool_step[e], 1)
                eng.wait_ge(pool_step[e], n + 1)
                eng.wait_ge(tile_affine, k + 1)
                TT(Pf[:, k], own, Y[:, k], ALU.subtract).then_inc(pooled[e], 1)
            else:
                TT(Pf[:, k], own, cnt[:], ALU.mult).then_inc(pooled[e], 1)

        @block.gpsimd
        def _(pool):
            TT = pool.tensor_tensor

            def lo_of_unit(s, n):
                pool.wait_ge(w_hi[s], n + 1)
                TT(W_lo[s][:], raw[s][:], W_hi[s][:].bitcast(F32), ALU.subtract).then_inc(w_ready[s], 1)

            def lo_of_odd(i, h):
                for k in range(1, KT, 2):
                    pool.wait_ge(h_hi, H_BASE[FILL[i]] + 8 * h + k + 1)
                    TT(H_lo[:, k, hs(h)], Y[:, k, hs(h)], H_hi[:, k, hs(h)].bitcast(F32), ALU.subtract)\
                        .then_inc(h_ready[1], 1)

            def odd_sum(q, h, p):
                n = 2 * q + h
                pool.wait_ge(sq_made, 8 * n + p + 1)
                if p > 3:
                    pool.wait_ge(sum_odd, 2 * n + p // 2 - 1)
                TT(acc[1][:, hs(h)], acc[1][:, hs(h)], S[1][:, hs(h)], ALU.add).then_inc(sum_odd, 1)

            def odd_sums(q, h):
                for p in (3, 5):
                    odd_sum(q, h, p)

            def odd_sum_whole(q, p):
                pool.wait_ge(sq_made, 16 * q + 2 * (p + 1))
                if p > 3:
                    pool.wait_ge(sum_odd, 4 * q + 2 * (p // 2 - 1))
                TT(acc[1][:], acc[1][:], S[1][:], ALU.add).then_inc(sum_odd, 2)

            def ada_products(p):
                for i in range(2):
                    pool.wait_ge(e_full[i], 16 * p + 16)
                    TT(E[i][:], E[i][:], silu_c[:, :, 0:1].to_broadcast([P, KT, P]), ALU.mult)\
                        .then_inc(e_mul, 1)

            def add_odd(i, h, ms):
                for m in ms:
                    if i == 0 and h == 0:
                        pool.wait_ge(res_full[m // 2], 16)
                    pool.wait_ge(y_scaled, 16 * i + 8 * h + m + 1)
                    TT(X[:, m, hs(h)], X[:, m, hs(h)], Y[:, m, hs(h)], ALU.add).then_inc(x_new[1], 1)

            def next_stream(q, i, lo):
                add_odd(i, 0, (1, 3, 5, 7))
                add_odd(i, 1, (1, 3))
                odd_sums(q + 1, 0)
                if lo:
                    lo(0)
                add_odd(i, 1, (5, 7))
                odd_sums(q + 1, 1)
                if lo:
                    lo(1)

            def fill_ffn(L, h):
                if h == 0:
                    pool.memset(Ub[:, 0:1], 0.0)
                    pool.memset(Ub[:, T + 1:T + 2], 0.0)
                lo_of_odd(1 + 2 * L, h)

            pool.memset(ones[:], 1.0).then_inc(memset_done, 1)
            pool.memset(eps[:], EPS).then_inc(memset_done, 1)
            pool.memset(s_exp[:], 0.0).then_inc(memset_done, 1)
            odd_sums(0, 0)
            odd_sums(0, 1)
            lo_of_unit("A", 0)
            lo_of_unit("B", 0)
            lo_of_odd(0, 0)
            pool.wait_ge(chi, 1)
            TT(Hc_lo[:], ctx_x[:], Hc_hi[:].bitcast(F32), ALU.subtract).then_inc(hc_ready, 1)
            lo_of_odd(0, 1)
            pool.wait_ge(hc_ready, 1)
            pool.wait_ge(rb_done, 2)
            for t in (rec[:, 0:2], rec[:, 2 + NC_:2 + LAT], rec[:, 2 + TA:3 + TA],
                      *(b[:, NC_:LAT] for b in (*RA, *IB))):
                ms = pool.memset(t, 0.0)
            ms.then_inc(zeros_ready, 1)

            def gated_lo(k):
                pool.wait_ge(h_hi, H_BASE[1] + k + 1)
                TT(H_lo[:, k], Y[:, k], H_hi[:, k].bitcast(F32), ALU.subtract).then_inc(gated_ready[1], 1)

            def head(hd, last=False):
                ada_products(2 * hd)
                lo_of_unit("A", hd + 1)
                pool.wait_ge(u_made, hd + 1)
                for d in range(2):
                    pool.wait_ge(gate_evac, 4 * hd + 2 * d + 2)
                    TT(IB[d][:], IB[d][:], u[:], ALU.mult).then_inc(iu_made, 1)
                    if d == 0 and not last:
                        ada_products(2 * hd + 1)
                if last:
                    gated_lo(1)
                lo_of_unit("B", hd + 1)

            head(0)
            with pool.Fori(1, NH - 1) as hd:
                head(hd)
            head(NH - 1, last=True)
            gated_lo(3)
            gated_lo(5)
            ada_products(2 * NH - 1)
            gated_lo(7)
            for m in range(KT):
                lo_of_unit("AB"[m % 2], NH + m // 2 + 1)
                if m in (3, 5):
                    odd_sum_whole(1, m)
            lo_of_unit("C", 0)

            def ffn_step(L, j):
                n, c = N_FFN[L] + j, FJ * L + j
                static = isinstance(j, int)
                last = static and j == FJ - 1
                if not last:
                    lo_of_unit("A", n + 1)
                if L == 0:
                    ada_products(2 * NH + j)
                if last:
                    pool.wait_ge(w_hi["C"], c + 1)
                    TT(W_lo["B"][:], raw["C"][:], W_hi["B"][:].bitcast(F32), ALU.subtract)\
                        .then_inc(w_ready["C"], 1)
                    return
                if not (static and c == 0):
                    lo_of_unit("C", c)
                pool.wait_ge(f_hi, c + 1 - L)
                TT(F_lo[:], S[1][:], F_hi[:].bitcast(F32), ALU.subtract).then_inc(f_ready, 1)
                lo_of_unit("B", n + 1)

            def ffn(L):
                ffn_step(L, 0)
                with pool.Fori(1, FJ - 1) as j:
                    ffn_step(L, j)
                ffn_step(L, FJ - 1)
                for h in range(2):
                    odd_sums(3 + 4 * L, h)

            next_stream(1, 0, lambda h: fill_ffn(0, h))
            ffn(0)
            next_stream(3, 1, None)
            pool.wait_ge(rb_done, 10)
            for grid in (col_p, row_p, col_v):
                pool.memset(grid[:], 0.0)
            pool.memset(row_v[:], 0.0).then_inc(pads_ready, 1)
            for t in range(4):
                pool_tile(pool, "p", t)
                if t == 0:
                    for s in "AB":
                        lo_of_unit(s, N_FFN[1])
            for p in (3, 5):
                odd_sum_whole(5, p)
            next_stream(5, 2, lambda h: fill_ffn(1, h))
            ffn(1)
            add_odd(3, 0, (1, 3, 5, 7))
            add_odd(3, 1, (1, 3, 5, 7))

        @block.vector
        def _(dve):
            TT, STT, TS = dve.tensor_tensor, dve.scalar_tensor_tensor, dve.tensor_scalar

            def even_sum(q, h, p):
                n = 2 * q + h
                dve.wait_ge(sq_made, 8 * n + p + 1)
                if p > 2:
                    dve.wait_ge(sum_even, 3 * n + p // 2 - 1)
                TT(acc[0][:, hs(h)], acc[0][:, hs(h)], S[0][:, hs(h)], ALU.add).then_inc(sum_even, 1)

            def even_sums(q, h):
                for p in range(2, KT, 2):
                    even_sum(q, h, p)
                last_sums(dve, 2 * q + h, hs(h), 1)

            def even_sums_whole(q):
                for p in range(2, KT, 2):
                    dve.wait_ge(sq_made, 16 * q + 2 * (p + 1))
                    if p > 2:
                        dve.wait_ge(sum_even, 6 * q + 2 * (p // 2 - 1))
                    TT(acc[0][:], acc[0][:], S[0][:], ALU.add).then_inc(sum_even, 2)
                last_sums(dve, 2 * q, slice(0, T), 2)

            def norm_diagonal(q, h):
                n, c = 2 * q + h, slice(4 * h, 4 * h + 4)
                dve.wait_ge(rms_made, n + 1)
                dve.reciprocal(rstd[:, c], rms[:, c]).then_inc(rstd_made, 1)
                dve.wait_ge(rstd_made, n + 1)
                if q:
                    dve.wait_ge(rb_done, n - 1)
                TT(diag[:, c], ident[:].unsqueeze(1).to_broadcast([P, 4, P]),
                   rstd[:, c].unsqueeze(2).to_broadcast([P, 4, P]), ALU.mult).then_inc(diag_made, 1)

            def ada_sums(p, at, n_used):
                dve.wait_ge(ada_out, n_used)
                for i in range(2):
                    dve.wait_ge(e_mul, 2 * p + i + 1)
                    dve.tensor_reduce(red[:, at + i], E[i][:].rearrange("p k m -> p m k"),
                                      mybir.AxisListType.X, ALU.add).then_inc(red_made, 1)

            def add_ada_bias(out, first, n, count):
                dve.wait_ge(ada_out, count)
                TT(M[:, bass.ds(first, n)], out, col("ada_b", first, n), ALU.add).then_inc(ada_added, 1)

            def coefs(i, L, ffn_part):
                a, o = 48 * L + 24 * ffn_part, 8 * L
                STT(cA[:, i], M[:, a + 8:a + 16], 1.0,
                    col(("npre_mix", "npre_ffn")[ffn_part], o, 8), ALU.add, ALU.mult)

            def gates(i, L, ffn_part):
                a, o = 48 * L + 24 * ffn_part, 8 * L
                return TT(cG[:, i], M[:, a + 16:a + 24], col(("npost_mix", "npost_ffn")[ffn_part], o, 8), ALU.mult)

            def scale_tiles(i, q, h, src, fill=True):
                dve.wait_ge(rb_done, 2 * q + h + 1)
                for k in range(KT + (4 if fill else 0)):
                    if k < KT:
                        STT(Y[:, k, hs(h)], src[:, k, hs(h)], cA[:, i, k:k + 1], ps[:, rb_bank(q, h)],
                            ALU.mult, ALU.mult).then_inc(x_scaled, 1)
                    if fill and k >= 4 and k % 2 == 0:
                        e = k - 4
                        c = {0: 0, 1: 24, 3: 72}[i] + e
                        dve.wait_ge(h_hi, H_BASE[FILL[i]] + 8 * h + e + 1)
                        STT(H_lo[:, e, hs(h)], Y[:, e, hs(h)], M[:, c:c + 1], H_hi[:, e, hs(h)].bitcast(F32),
                            ALU.add, ALU.subtract).then_inc(h_ready[0], 1)

            def gate_tiles(i, q, h, ms):
                dve.wait_ge(rb_done, 2 * q + h + 1)
                for m in ms:
                    STT(Y[:, m, hs(h)], Y[:, m, hs(h)], cG[:, i, m:m + 1], ps[:, rb_bank(q, h)],
                        ALU.mult, ALU.mult).then_inc(y_scaled, 1)
                    if m % 2:
                        if i == 0 and h == 0:
                            dve.wait_ge(res_full[m // 2], 16)
                        dve.wait_ge(y_scaled, 16 * i + 8 * h + m)
                        TT(X[:, m - 1, hs(h)], X[:, m - 1, hs(h)], Y[:, m - 1, hs(h)], ALU.add)\
                            .then_inc(x_new[0], 1)

            def next_stream(q, i, fill):
                if q != 3:
                    norm_diagonal(q, 0)
                    gate_tiles(i, q, 0, range(KT))
                norm_diagonal(q, 1)
                gate_tiles(i, q, 1, range(4))
                even_sums(q + 1, 0)
                norm_diagonal(q + 1, 0)
                scale_tiles(i + 1, q + 1, 0, X, fill)
                gate_tiles(i, q, 1, range(4, KT))
                even_sums(q + 1, 1)
                norm_diagonal(q + 1, 1)
                scale_tiles(i + 1, q + 1, 1, X, fill)

            dve.wait_ge(softplus_step, 2)
            TS(sp[:, 2], sp[:, 1], 1.0, None, ALU.add).then_inc(softplus_step, 1)
            dve.wait_ge(softplus_step, 4)
            TS(sp[:, 4], sp[:, 2], -1.0, None, ALU.add).then_inc(softplus_step, 1)
            dve.wait_ge(softplus_step, 5)
            TS(sp[:, 5], sp[:, 4], 0.0, None, ALU.is_equal).then_inc(softplus_step, 1)
            dve.wait_ge(softplus_step, 6)
            TT(sp[:, 3], sp[:, 3], sp[:, 5], ALU.add).then_inc(softplus_step, 1)
            TT(sp[:, 4], sp[:, 4], sp[:, 5], ALU.add).then_inc(softplus_step, 1)
            dve.wait_ge(softplus_step, 8)
            dve.reciprocal(sp[:, 6], sp[:, 4]).then_inc(softplus_step, 1)
            TT(sp[:, 3], sp[:, 3], sp[:, 1], ALU.mult).then_inc(softplus_step, 1)
            dve.wait_ge(softplus_step, 10)
            TT(sp[:, 3], sp[:, 3], sp[:, 6], ALU.mult).then_inc(softplus_step, 1)
            TS(sp[:, 7], col("lam", 0, 16), -1.0, 0.0, ALU.mult, ALU.max).then_inc(softplus_step, 1)
            dve.wait_ge(softplus_step, 12)
            TT(sp[:, 3], sp[:, 3], sp[:, 7], ALU.add).then_inc(softplus_step, 1)
            dve.wait_ge(softplus_step, 13)
            dve.wait_ge(memset_done, 3)
            TS(s_tanh[:], sp[:, 3], 0.5 * RG_C, None, ALU.mult)
            TS(s_exp[:], sp[:, 3], -RG_C, None, ALU.mult).then_inc(lam_ready, 1)
            TT(pbs[:], col("pool_b", 0, 8), col("pool_scale", 0, 8), ALU.mult)
            dve.wait_ge(const_full, 16)
            dve.wait_ge(crms_made, 1)
            dve.reciprocal(rstd_c[:], rms_c[:]).then_inc(crstd_made, 1)
            dve.wait_ge(crstd_made, 1)
            TT(diag_c[:], ident[:].unsqueeze(1).to_broadcast([P, 2, P]),
               rstd_c[:].unsqueeze(2).to_broadcast([P, 2, P]), ALU.mult).then_inc(cdiag_made, 1)
            dve.wait_ge(silu_done, 1)
            step = 0
            for q in (1, 3):
                dve.wait_ge(ada_first_full[q], 16)
                for k in range(KT):
                    for v in range(2):
                        rows, s_k = ada_first[:, 4 * q:4 * q + 4, k * P:k * P + P], silu_c[:, k, v:v + 1]
                        out = ada_part[:, v, 4 * (q // 2):4 * (q // 2) + 4]
                        if k == 0:
                            TS(out, rows, s_k, None, ALU.mult).then_inc(part_step, 1)
                        else:
                            dve.wait_ge(part_step, step - 1)
                            STT(out, rows, s_k, out, ALU.mult, ALU.add).then_inc(part_step, 1)
                        step += 1
                if q == 1:
                    dve.wait_ge(crb_done, 1)
                    TT(ctx_x[:], ctx_x[:], ps[:, 3, 0:NC_].unsqueeze(1).to_broadcast([P, KT, NC_]), ALU.mult)\
                        .then_inc(cscaled, 1)
            even_sums(0, 0)
            even_sums(0, 1)
            dve.wait_ge(ada_out, 1)
            first = ps[:, 2, 0:2 * ADA0].rearrange("p (m v) -> p m v", v=2)
            TT(M[:, 0:ADA0], first[:, :, 0], col("ada_b", 0, ADA0), ALU.add)
            TT(Mc[:], first[:, :, 1], col("ada_b", 0, ADA0), ALU.add).then_inc(ada_added, 1)
            dve.wait_ge(ada_added, 1)
            coefs(0, 0, 0)
            STT(cAc[:], Mc[:, 8:16], 1.0, col("npre_mix", 0, 8), ALU.add, ALU.mult).then_inc(coef_ready, 1)
            norm_diagonal(0, 0)
            dve.wait_ge(coef_ready, 1)
            dve.wait_ge(cscaled, 1)
            for k in range(KT):
                TS(ctx_x[:, k], ctx_x[:, k], cAc[:, k:k + 1], Mc[:, k:k + 1], ALU.mult, ALU.add)\
                    .then_inc(caffine, 1)
            norm_diagonal(0, 1)
            scale_tiles(0, 0, 0, Y)
            scale_tiles(0, 0, 1, Y)

            def convolve(hd):
                dve.wait_ge(rec_evac, hd + 1)
                if not (isinstance(hd, int) and hd == 0):
                    dve.wait_ge(gate_done, 4 * hd)
                    dve.wait_ge(iu_made, 2 * hd)
                TS(u[:], rec[:, 0:TA], col("rg_conv_w", hd), col("rg_conv_b", hd), ALU.mult, ALU.add)\
                    .then_inc(conv_step, 1)
                for tap in range(1, 4):
                    dve.wait_ge(conv_step, 3 * hd + tap)
                    STT(u[:], rec[:, tap:tap + TA], col("rg_conv_w", tap * NH + hd), u[:], ALU.mult, ALU.add)\
                        .then_inc(conv_step if tap < 3 else u_made, 1)

            def scans(hd, d):
                n = 2 * hd + d + 1
                dve.wait_ge(sqrt_made, n)
                STT(TH[d][:], RA[d][:], 1.0, TH[d][:], ALU.add, ALU.mult).then_inc(mult_made, 1)
                dve.wait_ge(mult_made, n)
                dve.wait_ge(iu_made, n)
                TT(IB[d][:], IB[d][:], TH[d][:], ALU.mult).then_inc(b_made, 1)
                dve.wait_ge(b_made, n)
                rev = slice(None, None, -1 if d else 1)
                a, b, h = ([t[:, 0:NC_][:, rev], t[:, LAT:TA][:, rev]] for t in (RA[d], IB[d], TH[d]))
                dve.tensor_tensor_scan(h[0], a[0], b[0], 0.0, ALU.mult, ALU.add).then_inc(scan_ctx, 1)
                dve.wait_ge(scan_ctx, n)
                dve.tensor_tensor_scan(h[1], a[1], b[1], h[0][:, NC_ - 1:NC_], ALU.mult, ALU.add)\
                    .then_inc(scan_done, 1)

            def combine(hd):
                dve.wait_ge(scan_done, 2 * hd + 2)
                TT(TH[0][:, LAT:TA], TH[0][:, LAT:TA], TH[1][:, LAT:TA], ALU.add).then_inc(ysum_made, 1)
                dve.wait_ge(ysum_made, hd + 1)
                dve.wait_ge(g_made, hd + 1)
                TT(Y[:, hd], Y[:, hd], TH[0][:, LAT:TA], ALU.mult).then_inc(gy_made, 1)

            def gated_lo(k):
                dve.wait_ge(h_hi, H_BASE[1] + k + 1)
                TT(H_lo[:, k], Y[:, k], H_hi[:, k].bitcast(F32), ALU.subtract).then_inc(gated_ready[0], 1)

            def head(hd, last=False):
                ada_sums(2 * hd, 0, hd + 1)
                if last:
                    gated_lo(0)
                    gated_lo(2)
                else:
                    ada_sums(2 * hd + 1, 2, hd + 1)
                scans(hd, 0)
                if not last:
                    convolve(hd + 1)
                    add_ada_bias(ps[:, 3, 0:4], ADA0 + 4 * hd, 4, hd + 2)
                else:
                    gated_lo(4)
                scans(hd, 1)
                combine(hd)
                if last:
                    gated_lo(6)
                    ada_sums(2 * hd + 1, 2, hd + 1)

            dve.wait_ge(zeros_ready, 1)
            convolve(0)
            head(0)
            with dve.Fori(1, NH - 1) as hd:
                head(hd)
            head(NH - 1, last=True)
            add_ada_bias(ps[:, 4, 0:4], ADA0 + 4 * (NH - 1), 4, NH + 1)
            dve.wait_ge(ada_added, NH + 1)
            coefs(1, 0, 1)
            gates(0, 0, 0)
            gates(1, 0, 1).then_inc(coef_ready, 1)
            even_sums_whole(1)
            dve.wait_ge(coef_ready, 2)
            next_stream(1, 0, True)

            def add_down(L, j):
                for m in range(KT):
                    dve.wait_ge(d_done, 8 * (FJ * L + j) + m + 1)
                    b = (4, 6, 0)[m % 3]
                    if isinstance(j, int) and j == 0:
                        dve.tensor_copy(Y[:, m], flat(ps[:, b:b + 2, :])).then_inc(d_added, 1)
                    else:
                        TT(Y[:, m], Y[:, m], flat(ps[:, b:b + 2, :]), ALU.add).then_inc(d_added, 1)

            def add_down_last(L):
                i, q = 1 + 2 * L, 3 + 4 * L
                for n in range(2 * KT):
                    h, m = divmod(n, KT)
                    dve.wait_ge(d_done, 8 * (FJ * (L + 1) - 2) + n + 1)
                    TT(Y[:, m, hs(h)], Y[:, m, hs(h)], ps[:, (6, 7, 0, 1, 4, 5)[n % 6]], ALU.add)\
                        .then_inc(d_added, 1)
                    if n in (4, 6, 8):
                        even_sum(q, 0, n - 2)
                    if n == 8:
                        last_sums(dve, 2 * q, hs(0), 1)
                    if n == 12:
                        norm_diagonal(q, 0)
                    if n in (12, 14):
                        even_sum(q, 1, n - 10)
                    if n == 14:
                        gate_tiles(i, q, 0, range(2))
                even_sum(q, 1, 6)
                last_sums(dve, 2 * q + 1, hs(1), 1)
                gate_tiles(i, q, 0, range(2, KT))

            def ffn_step(L, j):
                n, c = N_FFN[L] + j, FJ * L + j
                at0 = isinstance(j, int) and j == 0
                last = isinstance(j, int) and j == FJ - 1
                if not at0 and not last:
                    add_down(L, j - 1)
                dve.wait_ge(tap_done, c + 1)
                STT(S[0][:], Ub[:, 0:T], col("ffn_conv_w", 72 * L + j), S[0][:], ALU.mult, ALU.add)\
                    .then_inc(conv_a, 1)
                dve.wait_ge(conv_a, c + 1)
                STT(S[0][:], Ub[:, 2:T + 2], col("ffn_conv_w", 72 * L + 48 + j), S[0][:], ALU.mult, ALU.add)\
                    .then_inc(conv_done, 1)
                if L == 0:
                    ada_sums(2 * NH + j, 0, NH + 1 + j)
                dve.wait_ge(gelu_done, c + 1)
                dve.wait_ge(unit_done["B"], n + 1)
                if not (isinstance(c, int) and c == 0):
                    dve.wait_ge(f_ready, c - L)
                if last:
                    for h in range(2):
                        TT(S[1][:, hs(h)], S[0][:, hs(h)], ps[:, 2 + h], ALU.mult).then_inc(last_mul, 1)
                else:
                    TT(S[1][:], S[0][:], flat(AB23), ALU.mult).then_inc(f_mul, 1)
                if L == 0:
                    add_ada_bias(ps[:, 4, 0:2], 48 + 2 * j, 2, NH + 2 + j)
                if last:
                    for h in range(2):
                        dve.wait_ge(last_hi, 2 * L + h + 1)
                        TT(W_lo["A"][:, hs(h)], S[1][:, hs(h)], W_hi["A"][:, hs(h)].bitcast(F32),
                           ALU.subtract).then_inc(last_ready, 1)

            def ffn(L):
                ffn_step(L, 0)
                ffn_step(L, 1)
                with dve.Fori(2, FJ - 1) as j:
                    ffn_step(L, j)
                ffn_step(L, FJ - 1)
                add_down_last(L)

            ffn(0)
            dve.wait_ge(ada_added, NH + 1 + FJ)
            coefs(2, 1, 0)
            coefs(3, 1, 1)
            gates(2, 1, 0)
            gates(3, 1, 1).then_inc(coef_ready, 1)
            dve.wait_ge(coef_ready, 3)
            next_stream(3, 1, False)
            for t in range(4):
                pool_tile(dve, "v", t)
            even_sums_whole(5)
            next_stream(5, 2, True)
            ffn(1)
            norm_diagonal(7, 1)
            gate_tiles(3, 7, 1, range(KT))


def kernel(**inputs):
    import numpy as np
    import concourse.bacc as bacc
    from concourse.bass_utils import run_bass_kernel_spmd as run

    a = {k: np.asarray(v) for k, v in inputs.items()}

    def channel_major(x):
        return np.ascontiguousarray(x.reshape(x.shape[0], -1, P).transpose(2, 1, 0))

    def columns(v):
        return v.reshape(-1, P).T

    def out_tiles(w):
        return w.reshape(KT, P, -1, P).transpose(2, 1, 0, 3).reshape(-1, P, D)

    par = np.concatenate([columns(a[n]) for n in (
        "ada_b", "norm_pre_mix", "norm_post_mix", "norm_pre_ffn", "norm_post_ffn", "rg_conv_w", "rg_conv_b",
        "rg_gate_a_b", "rg_gate_x_b", "rg_lambda", "pool_b", "pool_scale", "ffn_conv_w", "ffn_conv_b")]
        + [np.stack([columns(a["c"]), columns(a["c_ctx"])], axis=-1).reshape(P, 16)], axis=1)
    w_in, w_out = out_tiles(a["rg_w_in"][0]), out_tiles(a["rg_w_out"][0])
    up = [out_tiles(a["ffn_w_up"][i]) for i in range(2)]
    down = a["ffn_w_down"].reshape(2 * FJ, P, D)
    pool = a["pool_w"][0].reshape(2, 2, 2, P, 256).transpose(0, 3, 1, 2, 4).reshape(2, P, D)
    slot_a = np.concatenate([w_in[NH:], w_out[0::2], up[0][:FJ], up[1][:FJ]])
    slot_b = np.concatenate([w_in[:NH], w_out[1::2], up[0][FJ:], up[1][FJ:]])
    gw = np.stack([a["rg_gate_a_w"][0], a["rg_gate_x_w"][0]], axis=1)
    gw = gw.transpose(2, 3, 0, 1, 4).reshape(NH, P, 4, P)
    ada = np.concatenate([out_tiles(a["ada_w"][i]) for i in range(2)])

    def reach(n, w):
        t = np.arange(n)
        return np.clip(t + w // 2, 0, n) - np.clip(t - w // 2, 0, n)

    cnt = np.stack([(1.0 / np.outer(reach(GR, w), reach(GW, w))).reshape(T) for w in WINDOWS]).astype(np.float32)
    arrays = {
        "xT": channel_major(a["x"][0]), "ctxT": channel_major(a["ctx"][0]), "params": par, "ada": ada,
        "wA": slot_a, "wB": slot_b, "wC": down, "gatew": gw, "poolw": pool, "poolcnt": cnt,
        "ident_in": np.eye(P, dtype=np.float32),
    }
    arrays = {k: np.ascontiguousarray(v) for k, v in arrays.items()}
    nc = bacc.Bacc("TRN2", target_bir_lowering=False, num_devices=1, dynamic_dma_scratch_size=1024)
    aps = [nc.dram_tensor(k, v.shape, F32, kind="ExternalInput").ap() for k, v in arrays.items()]
    out = nc.dram_tensor("outT", (P, KT, T), F32, kind="ExternalOutput").ap()
    build_trunk(nc, *aps, out)
    r = run(nc, [arrays], core_ids=[0])
    return r.results[0]["outT"].transpose(2, 1, 0).reshape(1, T, D)
```
